# Optimizing a Trainium2 kernel written in Bass

```python
import math
import jax, jax.numpy as jnp
from jax import lax
import numpy as np

D_MODEL = 1024
BATCH = 1
SEQ = 256
DEPTH = 2

F32 = jnp.float32
CHUNK = 64
N_EVEN = (DEPTH + 1) // 2
N_ODD = DEPTH // 2
NORM_EPS = 1e-6

A_Q_HEADS = 8
A_KV_HEADS = 2
A_GROUP = A_Q_HEADS // A_KV_HEADS
A_HEAD_DIM = D_MODEL // 16
A_WINDOW = 128
A_WINDOW_CHUNKS = A_WINDOW // CHUNK

B_HEADS = 4
B_DK = D_MODEL // 8
B_DV = D_MODEL // 8

C_HEADS = 8
C_DK = D_MODEL // 16
C_DV = D_MODEL // 16
C_CONV = 4

D_HEADS = 4
D_DK = D_MODEL // 16
D_DV = D_MODEL // 8
ROPE_BASE = 10000.0

MOE_GROUPS = 4
MOE_EXPERTS_PER_GROUP = 8
MOE_TOP_K = 2
MOE_HIDDEN = D_MODEL // 8

EVEN_SPLITS = (A_Q_HEADS * A_HEAD_DIM, A_KV_HEADS * A_HEAD_DIM, A_KV_HEADS * A_HEAD_DIM,
               B_HEADS * B_DK, B_HEADS * B_DK, B_HEADS * B_DV, B_HEADS * B_DV)
EVEN_IN = sum(EVEN_SPLITS)
EVEN_MIX = A_Q_HEADS * A_HEAD_DIM + B_HEADS * B_DV
C_QKV = C_HEADS * (2 * C_DK + C_DV)
ODD_SPLITS = (C_QKV, C_HEADS * C_DV, C_HEADS, C_HEADS,
              D_HEADS * D_DK, D_HEADS * D_DK, D_HEADS * D_DV, D_HEADS * D_DV)
ODD_IN = sum(ODD_SPLITS)
ODD_MIX = C_HEADS * C_DV + D_HEADS * D_DV

kernel_name = "hybrid_swa_hgrn2_gdn_retention_hmoe"

def _split(y, sizes):
    return jnp.split(y, [int(c) for c in np.cumsum(sizes)[:-1]], axis=-1)

def rms_norm(x, gain, eps=NORM_EPS):
    xf = x.astype(F32)
    y = xf * lax.rsqrt(jnp.mean(xf * xf, axis=-1, keepdims=True) + eps)
    return (y * gain.astype(F32)).astype(x.dtype)

def l2_norm(x, eps=NORM_EPS):
    return x * lax.rsqrt(jnp.sum(x * x, axis=-1, keepdims=True) + eps)

def head_group_norm(x, gain, bias, eps=NORM_EPS):
    mu = jnp.mean(x, axis=-1, keepdims=True)
    xc = x - mu
    var = jnp.mean(xc * xc, axis=-1, keepdims=True)
    return xc * lax.rsqrt(var + eps) * gain.astype(F32) + bias.astype(F32)

def to_chunks(x):
    b, s, h, d = x.shape
    return x.reshape(b, s // CHUNK, CHUNK, h, d).transpose(0, 3, 1, 2, 4)

def from_chunks(x):
    b, h, n, c, d = x.shape
    return x.transpose(0, 2, 3, 1, 4).reshape(b, n * c, h * d)

def rotary(x):
    s, d = x.shape[1], x.shape[-1]
    inv_freq = ROPE_BASE ** (-jnp.arange(0, d, 2, dtype=F32) / d)
    ang = jnp.arange(s, dtype=F32)[:, None] * inv_freq[None, :]
    cos, sin = jnp.cos(ang)[None, :, None, :], jnp.sin(ang)[None, :, None, :]
    x1, x2 = x[..., : d // 2], x[..., d // 2:]
    return jnp.concatenate([x1 * cos - x2 * sin, x1 * sin + x2 * cos], axis=-1)

def causal_depthwise_conv(x, w):
    k, ch = w.shape
    return lax.conv_general_dilated(x, w[:, None, :], window_strides=(1,), padding=((k - 1, 0),),
                                    dimension_numbers=('NWC', 'WIO', 'NWC'), feature_group_count=ch)

def sliding_window_sink_attention(q, k, v, q_gain, k_gain, sinks):
    b, s, _ = q.shape
    n = s // CHUNK
    q = rms_norm(q.reshape(b, s, A_Q_HEADS, A_HEAD_DIM), q_gain).astype(F32)
    k = rms_norm(k.reshape(b, s, A_KV_HEADS, A_HEAD_DIM), k_gain).astype(F32)
    v = v.reshape(b, s, A_KV_HEADS, A_HEAD_DIM).astype(F32)
    qb = q.reshape(b, n, CHUNK, A_KV_HEADS, A_GROUP, A_HEAD_DIM)
    kb = k.reshape(b, n, CHUNK, A_KV_HEADS, A_HEAD_DIM)
    vb = v.reshape(b, n, CHUNK, A_KV_HEADS, A_HEAD_DIM)
    pad = ((0, 0), (A_WINDOW_CHUNKS - 1, 0), (0, 0), (0, 0), (0, 0))
    kp, vp = jnp.pad(kb, pad), jnp.pad(vb, pad)
    kw = jnp.concatenate([kp[:, j:j + n] for j in range(A_WINDOW_CHUNKS)], axis=2)
    vw = jnp.concatenate([vp[:, j:j + n] for j in range(A_WINDOW_CHUNKS)], axis=2)
    key_chunk = (jnp.arange(n)[:, None] - (A_WINDOW_CHUNKS - 1)
                 + jnp.arange(A_WINDOW_CHUNKS * CHUNK)[None, :] // CHUNK)
    valid = key_chunk >= 0
    scores = jnp.einsum('bncgrd,bnkgd->bngrck', qb, kw) * (A_HEAD_DIM ** -0.5)
    scores = jnp.where(valid[None, :, None, None, None, :], scores, -1e30)
    sink = jnp.broadcast_to(sinks.astype(F32).reshape(A_KV_HEADS, A_GROUP)[None, None, :, :, None, None],
                            scores.shape[:-1] + (1,))
    probs = jax.nn.softmax(jnp.concatenate([scores, sink], axis=-1), axis=-1)[..., :-1]
    out = jnp.einsum('bngrck,bnkgd->bncgrd', probs, vw)
    return out.reshape(b, s, A_Q_HEADS * A_HEAD_DIM)

def hgrn2_recurrence(q, f_logit, i, g, lower_bound, out_gain):
    b, s, _ = q.shape
    lb = lower_bound.astype(F32)
    f = lb + (1.0 - lb) * jax.nn.sigmoid(f_logit.astype(F32))
    qh = jax.nn.silu(q.astype(F32)).reshape(b, s, B_HEADS, B_DK)
    kh = (1.0 - f).reshape(b, s, B_HEADS, B_DK)
    log_f = jnp.log(f).reshape(b, s, B_HEADS, B_DK)
    vh = i.astype(F32).reshape(b, s, B_HEADS, B_DV)
    qc, kc, vc = to_chunks(qh), to_chunks(kh), to_chunks(vh)
    bc = jnp.cumsum(to_chunks(log_f), axis=3)
    causal = jnp.tril(jnp.ones((CHUNK, CHUNK), bool))[:, :, None]

    def step(state, xs):
        qi, ki, vi, bi = xs
        diff = bi[:, :, :, None, :] - bi[:, :, None, :, :]
        decay = jnp.where(causal, jnp.exp(jnp.where(causal, diff, 0.0)), 0.0)
        attn = jnp.sum(qi[:, :, :, None, :] * ki[:, :, None, :, :] * decay, axis=-1)
        o = (jnp.einsum('bhts,bhsv->bhtv', attn, vi)
             + jnp.einsum('bhtd,bhdv->bhtv', qi * jnp.exp(bi), state))
        b_last = bi[:, :, -1:, :]
        state = (jnp.exp(b_last[:, :, 0, :, None]) * state
                 + jnp.einsum('bhsd,bhsv->bhdv', ki * jnp.exp(b_last - bi), vi))
        return state, o

    xs = tuple(jnp.moveaxis(t, 2, 0) for t in (qc, kc, vc, bc))
    init = jnp.zeros((b, B_HEADS, B_DK, B_DV), F32)
    _, o = lax.scan(step, init, xs)
    o = from_chunks(jnp.moveaxis(o, 0, 2)).reshape(b, s, B_HEADS, B_DV)
    o = rms_norm(o, out_gain) * jax.nn.silu(g.astype(F32)).reshape(b, s, B_HEADS, B_DV)
    return o.reshape(b, s, B_HEADS * B_DV)

def gated_deltanet(qkv, z, beta_logit, a, conv_w, a_log, dt_bias, out_gain):
    b, s, _ = qkv.shape
    qkv = jax.nn.silu(causal_depthwise_conv(qkv.astype(F32), conv_w.astype(F32)))
    q, k, v = _split(qkv, (C_HEADS * C_DK, C_HEADS * C_DK, C_HEADS * C_DV))
    q = l2_norm(q.reshape(b, s, C_HEADS, C_DK)) * (C_DK ** -0.5)
    k = l2_norm(k.reshape(b, s, C_HEADS, C_DK))
    v = v.reshape(b, s, C_HEADS, C_DV)
    beta = jax.nn.sigmoid(beta_logit.astype(F32))
    g = -jnp.exp(a_log.astype(F32)) * jax.nn.softplus(a.astype(F32) + dt_bias.astype(F32))
    qc, kc, vc = to_chunks(q), to_chunks(k), to_chunks(v)
    betac = to_chunks(beta[..., None])[..., 0]
    bc = jnp.cumsum(to_chunks(g[..., None])[..., 0], axis=-1)
    causal = jnp.tril(jnp.ones((CHUNK, CHUNK), bool))
    strict = jnp.tril(jnp.ones((CHUNK, CHUNK), bool), k=-1)
    diff = bc[..., :, None] - bc[..., None, :]
    gam = jnp.where(causal, jnp.exp(jnp.where(causal, diff, 0.0)), 0.0)
    kk = jnp.einsum('bhntd,bhnsd->bhnts', kc, kc)
    m = jnp.where(strict, betac[..., :, None] * kk * gam, 0.0)
    rhs = jnp.concatenate([vc * betac[..., None], kc * (betac * jnp.exp(bc))[..., None]], axis=-1)
    sol = lax.linalg.triangular_solve(m + jnp.eye(CHUNK, dtype=F32), rhs, left_side=True,
                                      lower=True, unit_diagonal=True)
    u, w = sol[..., :C_DV], sol[..., C_DV:]
    qk = jnp.einsum('bhntd,bhnsd->bhnts', qc, kc) * gam
    q_dec = qc * jnp.exp(bc)[..., None]
    k_dec = kc * jnp.exp(bc[..., -1:] - bc)[..., None]
    g_last = jnp.exp(bc[..., -1])

    def step(state, xs):
        u_i, w_i, qk_i, qd_i, kd_i, gl_i = xs
        v_new = u_i - jnp.einsum('bhtd,bhdv->bhtv', w_i, state)
        o = jnp.einsum('bhtd,bhdv->bhtv', qd_i, state) + jnp.einsum('bhts,bhsv->bhtv', qk_i, v_new)
        state = gl_i[..., None, None] * state + jnp.einsum('bhsd,bhsv->bhdv', kd_i, v_new)
        return state, o

    xs = tuple(jnp.moveaxis(t, 2, 0) for t in (u, w, qk, q_dec, k_dec, g_last))
    init = jnp.zeros((b, C_HEADS, C_DK, C_DV), F32)
    _, o = lax.scan(step, init, xs)
    o = from_chunks(jnp.moveaxis(o, 0, 2)).reshape(b, s, C_HEADS, C_DV)
    o = rms_norm(o, out_gain) * jax.nn.silu(z.astype(F32)).reshape(b, s, C_HEADS, C_DV)
    return o.reshape(b, s, C_HEADS * C_DV)

def retention(q, k, v, g, out_gain, out_bias):
    b, s, _ = q.shape
    q = rotary(q.astype(F32).reshape(b, s, D_HEADS, D_DK))
    k = rotary(k.astype(F32).reshape(b, s, D_HEADS, D_DK)) * (D_DK ** -0.5)
    v = v.astype(F32).reshape(b, s, D_HEADS, D_DV)
    log_gamma = jnp.log(1.0 - 2.0 ** (-5.0 - jnp.arange(D_HEADS, dtype=F32)))
    pos = jnp.arange(CHUNK, dtype=F32)
    rel = pos[:, None] - pos[None, :]
    decay = jnp.where(rel >= 0, jnp.exp(jnp.where(rel >= 0, rel, 0.0)[None] * log_gamma[:, None, None]), 0.0)
    qc, kc, vc = to_chunks(q), to_chunks(k), to_chunks(v)
    attn = jnp.einsum('bhntd,bhnsd->bhnts', qc, kc) * decay[None, :, None]
    o_intra = jnp.einsum('bhnts,bhnsv->bhntv', attn, vc)
    k_scale = jnp.exp((CHUNK - 1 - pos)[None, :] * log_gamma[:, None])
    kv = jnp.einsum('bhnsd,bhnsv->bhndv', kc * k_scale[None, :, None, :, None], vc)
    chunk_decay = jnp.exp(CHUNK * log_gamma)[None, :, None, None]

    def step(state, kv_i):
        return chunk_decay * state + kv_i, state

    _, r_prev = lax.scan(step, jnp.zeros((b, D_HEADS, D_DK, D_DV), F32), jnp.moveaxis(kv, 2, 0))
    r_prev = jnp.moveaxis(r_prev, 0, 2)
    q_scale = jnp.exp((pos + 1.0)[None, :] * log_gamma[:, None])
    o_inter = jnp.einsum('bhntd,bhndv->bhntv', qc * q_scale[None, :, None, :, None], r_prev)
    o = from_chunks(o_intra + o_inter).reshape(b, s, D_HEADS, D_DV)
    o = head_group_norm(o, out_gain, out_bias) * jax.nn.silu(g.astype(F32)).reshape(b, s, D_HEADS, D_DV)
    return o.reshape(b, s, D_HEADS * D_DV)

def even_layer_mixer(h, w_in, w_out, a_q_gain, a_k_gain, a_sinks, b_lower_bound, b_out_gain):
    a_q, a_k, a_v, b_q, b_f, b_i, b_g = _split(h @ w_in, EVEN_SPLITS)
    o_a = sliding_window_sink_attention(a_q, a_k, a_v, a_q_gain, a_k_gain, a_sinks)
    o_b = hgrn2_recurrence(b_q, b_f, b_i, b_g, b_lower_bound, b_out_gain)
    return jnp.concatenate([o_a, o_b], axis=-1).astype(h.dtype) @ w_out

def odd_layer_mixer(h, w_in, w_out, c_conv_w, c_a_log, c_dt_bias, c_out_gain, d_out_gain, d_out_bias):
    c_qkv, c_z, c_beta, c_a, d_q, d_k, d_v, d_g = _split(h @ w_in, ODD_SPLITS)
    o_c = gated_deltanet(c_qkv, c_z, c_beta, c_a, c_conv_w, c_a_log, c_dt_bias, c_out_gain)
    o_d = retention(d_q, d_k, d_v, d_g, d_out_gain, d_out_bias)
    return jnp.concatenate([o_c, o_d], axis=-1).astype(h.dtype) @ w_out

def hierarchical_moe(h, w_rg, b_rg, w_re, b_re, w_gate, w_up, w_down):
    b, s, d = h.shape
    t = h.reshape(b * s, d)
    p_group = jax.nn.softmax((t @ w_rg).astype(F32) + b_rg.astype(F32), axis=-1)
    p_g_top, g_idx = lax.top_k(p_group, 1)
    logits_e = ((t @ w_re).astype(F32) + b_re.astype(F32)).reshape(-1, MOE_GROUPS, MOE_EXPERTS_PER_GROUP)
    logits_sel = jnp.take_along_axis(logits_e, g_idx[:, :, None], axis=1)[:, 0]
    p_e_top, e_idx = lax.top_k(jax.nn.softmax(logits_sel, axis=-1), MOE_TOP_K)
    w_top = p_g_top * p_e_top / jnp.sum(p_e_top, axis=-1, keepdims=True)
    expert_w = jnp.sum(jax.nn.one_hot(e_idx, MOE_EXPERTS_PER_GROUP, dtype=F32) * w_top[..., None], axis=1)
    gate = jax.nn.one_hot(g_idx[:, 0], MOE_GROUPS, dtype=F32)[:, :, None] * expert_w[:, None, :]
    out = jnp.zeros((b * s, d), F32)
    for grp in range(MOE_GROUPS):
        hid = (jax.nn.silu(jnp.einsum('td,edf->tef', t, w_gate[grp]))
               * jnp.einsum('td,edf->tef', t, w_up[grp]))
        out = out + jnp.einsum('tef,efd->td', hid * gate[:, grp, :, None].astype(hid.dtype), w_down[grp])
    return out.reshape(b, s, d).astype(h.dtype)

def setup_inputs(seed: int = 0) -> dict:
    key = jax.random.key(seed)
    ks = iter(jax.random.split(key, 32))

    def normal(shape, scale):
        return jax.random.normal(next(ks), shape, F32) * scale

    x = normal((BATCH, SEQ, D_MODEL), 1.0)
    mix_norm = 1.0 + normal((DEPTH, D_MODEL), 0.02)
    moe_norm = 1.0 + normal((DEPTH, D_MODEL), 0.02)
    ev_w_in = normal((N_EVEN, D_MODEL, EVEN_IN), D_MODEL ** -0.5)
    ev_w_out = normal((N_EVEN, EVEN_MIX, D_MODEL), EVEN_MIX ** -0.5)
    a_q_gain = 1.0 + normal((N_EVEN, A_HEAD_DIM), 0.02)
    a_k_gain = 1.0 + normal((N_EVEN, A_HEAD_DIM), 0.02)
    a_sinks = normal((N_EVEN, A_Q_HEADS), 0.5)
    b_lb_logits = normal((DEPTH + 1, B_HEADS * B_DK), 0.1)
    b_out_gain = 1.0 + normal((N_EVEN, B_DV), 0.02)
    od_w_in = normal((N_ODD, D_MODEL, ODD_IN), D_MODEL ** -0.5)
    od_w_out = normal((N_ODD, ODD_MIX, D_MODEL), ODD_MIX ** -0.5)
    c_conv_w = normal((N_ODD, C_CONV, C_QKV), C_CONV ** -0.5)
    c_a_log = jnp.log(jax.random.uniform(next(ks), (N_ODD, C_HEADS), F32, minval=1.0, maxval=16.0))
    dt = jnp.exp(jax.random.uniform(next(ks), (N_ODD, C_HEADS), F32,
                                    minval=math.log(1e-3), maxval=math.log(1e-1)))
    c_dt_bias = dt + jnp.log(-jnp.expm1(-dt))
    c_out_gain = 1.0 + normal((N_ODD, C_DV), 0.02)
    d_out_gain = 1.0 + normal((N_ODD, D_HEADS, D_DV), 0.02)
    d_out_bias = normal((N_ODD, D_HEADS, D_DV), 0.02)
    moe_w_rg = normal((DEPTH, D_MODEL, MOE_GROUPS), D_MODEL ** -0.5)
    moe_b_rg = normal((DEPTH, MOE_GROUPS), 0.01)
    moe_w_re = normal((DEPTH, D_MODEL, MOE_GROUPS * MOE_EXPERTS_PER_GROUP), D_MODEL ** -0.5)
    moe_b_re = normal((DEPTH, MOE_GROUPS * MOE_EXPERTS_PER_GROUP), 0.01)
    moe_w_gate = normal((DEPTH, MOE_GROUPS, MOE_EXPERTS_PER_GROUP, D_MODEL, MOE_HIDDEN), D_MODEL ** -0.5)
    moe_w_up = normal((DEPTH, MOE_GROUPS, MOE_EXPERTS_PER_GROUP, D_MODEL, MOE_HIDDEN), D_MODEL ** -0.5)
    moe_w_down = normal((DEPTH, MOE_GROUPS, MOE_EXPERTS_PER_GROUP, MOE_HIDDEN, D_MODEL), MOE_HIDDEN ** -0.5)
    return {"x": x, "mix_norm": mix_norm, "moe_norm": moe_norm,
            "ev_w_in": ev_w_in, "ev_w_out": ev_w_out, "a_q_gain": a_q_gain, "a_k_gain": a_k_gain,
            "a_sinks": a_sinks, "b_lb_logits": b_lb_logits, "b_out_gain": b_out_gain,
            "od_w_in": od_w_in, "od_w_out": od_w_out, "c_conv_w": c_conv_w, "c_a_log": c_a_log,
            "c_dt_bias": c_dt_bias, "c_out_gain": c_out_gain, "d_out_gain": d_out_gain,
            "d_out_bias": d_out_bias, "moe_w_rg": moe_w_rg, "moe_b_rg": moe_b_rg,
            "moe_w_re": moe_w_re, "moe_b_re": moe_b_re, "moe_w_gate": moe_w_gate,
            "moe_w_up": moe_w_up, "moe_w_down": moe_w_down}

def reference(x, mix_norm, moe_norm, ev_w_in, ev_w_out, a_q_gain, a_k_gain, a_sinks, b_lb_logits,
              b_out_gain, od_w_in, od_w_out, c_conv_w, c_a_log, c_dt_bias, c_out_gain, d_out_gain,
              d_out_bias, moe_w_rg, moe_b_rg, moe_w_re, moe_b_re, moe_w_gate, moe_w_up, moe_w_down):
    lower_bounds = jnp.cumsum(jax.nn.softmax(b_lb_logits.astype(F32), axis=0), axis=0)
    for layer in range(DEPTH):
        h = rms_norm(x, mix_norm[layer])
        if layer % 2 == 0:
            i = layer // 2
            mix = even_layer_mixer(h, ev_w_in[i], ev_w_out[i], a_q_gain[i], a_k_gain[i], a_sinks[i],
                                   lower_bounds[layer], b_out_gain[i])
        else:
            i = layer // 2
            mix = odd_layer_mixer(h, od_w_in[i], od_w_out[i], c_conv_w[i], c_a_log[i], c_dt_bias[i],
                                  c_out_gain[i], d_out_gain[i], d_out_bias[i])
        x = x + mix.astype(x.dtype)
        h = rms_norm(x, moe_norm[layer])
        x = x + hierarchical_moe(h, moe_w_rg[layer], moe_b_rg[layer], moe_w_re[layer], moe_b_re[layer],
                                 moe_w_gate[layer], moe_w_up[layer], moe_w_down[layer])
    return x


_drawn_inputs = setup_inputs


def setup_inputs(seed=0):
    import zlib

    import numpy as np

    out = dict(_drawn_inputs(seed))
    spreads = {}
    factors = {'a_q_gain': 3.216,
     'a_k_gain': 2.899,
     'a_sinks': 200.0,
     'c_out_gain': 90.422,
     'd_out_gain': 80.346,
     'd_out_bias': 85.157,
     'moe_b_rg': 3.295,
     'b_lb_logits': 3.456,
     'moe_b_re': 4.125}
    for name, (base, spread) in spreads.items():
        noise = np.random.default_rng([zlib.crc32(name.encode()), seed]).standard_normal(out[name].shape)
        drawn = base * np.exp(spread * noise) if base else spread * noise
        out[name] = __import__('jax').numpy.asarray(drawn.astype(out[name].dtype))
    for name, factor in factors.items():
        out[name] = (out[name] * factor).astype(out[name].dtype)
    return out
```

```python
from contextlib import ExitStack

import numpy as np
import concourse.bass as bass
from concourse import mybir

F32 = mybir.dt.float32
F32R = mybir.dt.float32r
U8 = mybir.dt.uint8
ALU = mybir.AluOpType
ACT = mybir.ActivationFunctionType
AX = mybir.AxisListType.X

P = 128
T = 256
NT = T // P
D = 1024
KT = D // P
CH = 64
EPS = 1e-6
NEG = -1e30
EVEN_IN, ODD_IN = 2816, 3600
G, E = 4, 8
SLOTS = 4
SLOT = 3 * D
UNITS = 6
UNIT = D

C_ID, C_TRIU, C_SLOW, C_STRIU, C_ONES, C_NEG, C_IOTA = (i * P for i in range(7))
C_DEC = 7 * P
C_COS = C_DEC + 4 * T
C_SIN = C_COS + 64
C_SEL = C_SIN + 64
C_LOW8 = C_SEL + 2
C_LOW4 = C_LOW8 + 64
C_HEAD = C_LOW4 + 16
C_END = C_HEAD + 512
LEVELS = (1, 2, 4, 8, 16, 32, 64)
OV_DVE = 6 * E + 7


def constant_table():
    c = np.zeros((P, C_END), np.float32)
    s, t = np.arange(P)[:, None], np.arange(P)[None, :]
    c[:, C_ID:C_ID + P] = s == t
    c[:, C_TRIU:C_TRIU + P] = s <= t
    c[:, C_SLOW:C_SLOW + P] = s > t
    c[:, C_STRIU:C_STRIU + P] = s < t
    c[:, C_ONES:C_ONES + P] = 1.0
    c[:, C_NEG:C_NEG + P] = np.where(s <= t, 0.0, NEG)
    c[:, C_IOTA:C_IOTA + P] = t
    tt = np.arange(T)[None, :]
    for h in range(4):
        log_gamma = np.log(1.0 - 2.0 ** (-5.0 - h))
        dec = np.where(tt >= s, np.exp(np.maximum(tt - s, 0) * log_gamma), 0.0) * 64.0 ** -0.5
        c[:, C_DEC + h * T:C_DEC + (h + 1) * T] = dec
    freq = (10000.0 ** (-np.arange(0, 64, 2, dtype=np.float32) / 64)).astype(np.float32)
    for i in range(NT):
        ang = (np.arange(P, dtype=np.float32)[:, None] + i * P) * freq[None, :]
        c[:, C_COS + 32 * i:C_COS + 32 * (i + 1)] = np.cos(ang)
        c[:, C_SIN + 32 * i:C_SIN + 32 * (i + 1)] = np.sin(ang)
    c[:, C_SEL] = np.arange(P) < 64
    c[:, C_SEL + 1] = np.arange(P) >= 64
    c[:, C_LOW8:C_LOW8 + 64] = (np.arange(8)[None, :] < np.arange(8)[:, None]).ravel()
    c[:, C_LOW4:C_LOW4 + 16] = (np.arange(4)[None, :] < np.arange(4)[:, None]).ravel()
    c[:, C_HEAD:C_HEAD + 512] = np.arange(512)[None, :] // 64 == np.arange(P)[:, None]
    return c


def level_masks():
    s, t = np.arange(P)[:, None], np.arange(P)[None, :]
    return np.stack([(s // (2 * h) == t // (2 * h)) & (s % (2 * h) < h) & (t % (2 * h) >= h)
                     for h in LEVELS], 1).astype(np.float32)


EVEN_CHUNKS = [("feat", 768, 384), ("feat", 1152, 384), ("feat", 1536, 256),
               ("tok", 0, 384), ("tok", 384, 384),
               ("tok", 1792, 384), ("tok", 2176, 384), ("tok", 2560, 256)]
ODD_CHUNKS = [("feat", 0, 384), ("feat", 384, 384), ("feat", 768, 384), ("feat", 1152, 384),
              ("tok", 1536, 384), ("tok", 1920, 384), ("tok", 2304, 384), ("tok", 2688, 384),
              ("tok", 3072, 384), ("tok", 3456, 144)]
OUT_CHUNKS = [("tok", 0, 384), ("tok", 384, 384), ("tok", 768, 256)]


def program(nc, x, mix_norm, moe_norm, ev_w_in, ev_w_out, a_q_gain, a_k_gain, a_sinks, b_lb_logits,
            b_out_gain, od_w_in, od_w_out, c_conv_w, c_a_log, c_dt_bias, c_out_gain, d_out_gain,
            d_out_bias, moe_w_rg, moe_b_rg, moe_w_re, moe_b_re, moe_w_gate, moe_w_up, moe_w_down,
            consts, masks, out, stop=4):
    ctx = ExitStack()
    with ctx:
        base = (nc.sbuf_base + 31) // 32 * 32
        top = [base]

        def at(name, shape, off, dt=F32):
            return nc.alloc_sbuf_tensor_at(name, shape, dt, offset=off)

        def size(shape, dt=F32):
            n = 1
            for v in shape[1:]:
                n *= v
            return (n * (1 if dt == U8 else 4) + 31) // 32 * 32

        def sb(name, shape, dt=F32):
            off = top[0]
            top[0] += size(shape, dt)
            return at(name, shape, off, dt)

        RAW = sb("RAW", [P, SLOTS, SLOT])
        ov = top[0]
        WH = sb("WH", [P, UNITS, UNIT], F32R)
        WL = sb("WL", [P, UNITS, UNIT], F32R)
        X = sb("X", [P, NT, D])
        CT = sb("CT", [P, C_END])
        MK = sb("MK", [P, len(LEVELS), P], U8)
        ROWS = sb("ROWS", [P, P])
        PT = sb("PT", [P, 64])
        BC = sb("BC", [P, 8 + 128 + 64 + 8 + 8 + 72])
        RW = sb("RW", [P, 2, KT, G + G * E])
        SM = sb("SM", [P, 512])
        OVI = sb("OVI", [P, 2, 2], mybir.dt.int32)
        GB = sb("GB", [P, D])
        arena = top[0]
        SINK, BGAIN, CGAIN = BC[:, 0:8], BC[:, 8:136], BC[:, 136:200]
        ALOG, DTB = BC[:, 200:208], BC[:, 208:216]
        RB = BC[:, 216:288].rearrange("p (l n) -> p l n", l=2)
        ident = CT[:, C_ID:C_ID + P]

        def mask(level):
            return MK[:, level, :]

        class Map:

            def __init__(self, start, end):
                self.at, self.end = start, end

            def take(self, name, shape, dt=F32):
                t = at(name, shape, self.at, dt)
                self.at += size(shape, dt)
                assert self.at <= self.end, (name, self.at, self.end)
                return t

        END = nc.sbuf_base + nc.sbuf_bytes_remaining
        m = Map(arena, END)
        ht = m.at
        HTH = m.take("HTH", [P, KT, T], F32R)
        HTL = m.take("HTL", [P, KT, T], F32R)
        hh = m.at
        H = m.take("H", [P, NT, D])
        mix = m.at
        MKF = at("MKF", [P, len(LEVELS), P], mix)
        m = Map(mix, END)
        TA = m.take("TA", [P, NT, 768])
        TB = m.take("TB", [P, NT, 1024])
        TQ = m.take("TQ", [P, 4, T])
        QR = m.take("QR", [P, 4, T])
        TF = m.take("TF", [P, 4, T])
        KH = m.take("KH", [P, 4, T])
        LB = m.take("LB", [P, 4, T])
        DL = m.take("DL", [P, 2, 4 * T])
        ML = m.take("ML", [P, 2, 4 * T])
        m = Map(ov, ov + 2 * UNITS * UNIT * 4)
        KD = m.take("KD", [P, NT, 2, 2, 64])
        VS = m.take("VS", [P, 128])
        QT = m.take("QT", [P, 4, T])
        KTT = m.take("KTT", [P, 2, T])
        SB = m.take("SB", [P, NT, 8, P])
        PTS = m.take("PTS", [P, NT, 8, P])
        AT = m.take("AT", [P, NT, 4, P])
        AXB = m.take("AXB", [P, 4, P])
        SQB = m.take("SQB", [P, NT, 4, P])
        m = Map(ht, mix)
        TG = m.take("TG", [P, NT, 512])
        RST = m.take("RST", [P, 4 * T])
        m = Map(mix, END)
        TM = m.take("TM", [P, NT, 2064])
        cb = m.at
        CB = m.take("CB", [P, 12, T + 4])
        sl = m.at
        SL = m.take("SL", [P, 12, T])
        VB = m.take("VB", [P, NT, 8, 64])
        U = m.take("U", [P, NT, 8, 64])
        R1 = m.take("R1", [P, 8, 64])
        DG = m.take("DG", [P, 512])
        DB = m.take("DB", [P, 512])
        m = Map(ht, hh)
        QH = m.take("QH", [P, 4, T])
        KHC = m.take("KHC", [P, 4, T])
        KB = m.take("KB", [P, 4, T])
        SG = m.take("SG", [P, NT, 512])
        YI = at("YI", [P, NT, 8, P], hh)
        ATD = at("ATD", [P, 4, 384], hh)
        XI = at("XI", [P, NT, 8, P], cb)
        SQC = at("SQC", [P, 8, T], cb)
        QI = at("QI", [P, NT, 8, P], sl)
        m = Map(ov, ov + 2 * UNITS * UNIT * 4)
        GA = m.take("GA", [P, 8, 384])
        NTD = m.take("NTD", [P, 8, 384])
        ATC = m.take("ATC", [P, 8, 384])
        od = m.at
        QRD = m.take("QRD", [P, NT, 8, 64])
        TMP = m.take("TMP", [P, NT, 8, 64])
        qt = m.at
        QTD = m.take("QTD", [P, 4, T])
        SQD = at("SQD", [P, NT, 512], qt)
        m = Map(ht, hh)
        GTH = m.take("GTH", [P, 2, KT, P], F32R)
        GTL = m.take("GTL", [P, 2, KT, P], F32R)
        m = Map(mix, END)
        HH = m.take("HH", [P, NT, D], F32R)
        HL = m.take("HL", [P, NT, D], F32R)
        HTF = m.take("HTF", [P, KT, T])
        PF = m.take("PF", [P, NT, G, P])
        PR = m.take("PR", [P, NT, G, P], F32R)
        PTR = m.take("PTR", [P, G, T])
        GG = m.take("GG", [P, G * E])
        SIL = m.take("SIL", [P, 2, P])
        HID = m.take("HID", [P, 2, P])
        HIH = m.take("HIH", [P, 2, P], F32R)
        HIL = m.take("HIL", [P, 2, P], F32R)
        YS = m.take("YS", [P, D])
        MW = m.take("MW", [P, 1600])

        PS = ctx.enter_context(nc.psum_tensor("PS", [P, 8, 512], F32))

        sems = {}
        cnt = {}

        def sem(name):
            if name not in sems:
                sems[name] = ctx.enter_context(nc.semaphore(name))
            return sems[name]

        def done(ins, name, n=1):
            ins.then_inc(sem(name), n)
            cnt[name] = cnt.get(name, 0) + n
            return cnt[name]

        def linker(eng, name):
            def link(ins, also=None):
                if also is not None:
                    eng.wait_ge(sem(also), done(ins, also))
                else:
                    eng.wait_ge(sem(name), done(ins, name))
            return link

        plan = []
        for layer, chunks in ((0, EVEN_CHUNKS), (1, ODD_CHUNKS)):
            plan += [(layer, "in", c, 4) for c in range(len(chunks))]
            plan += [(layer, "out", c, 4) for c in range(3)]
            plan += [(layer, "moe", c, 3) for c in range(G * E)]
        slot_of, unit_of, u = {}, {}, 0
        for i, (layer, what, c, n) in enumerate(plan):
            slot_of[layer, what, c] = i
            unit_of[layer, what, c] = u
            u += n
        units_before = [unit_of[a, b, c] for a, b, c, _ in plan] + [u]
        limit = {0: 0, 1: slot_of[0, "moe", 0], 2: slot_of[1, "in", 0], 3: slot_of[1, "moe", 0], 4: len(plan)}[stop]

        block = ctx.enter_context(nc.Block())
        CHUNKS = (EVEN_CHUNKS, ODD_CHUNKS)

        outs_before = {}
        o = 0
        for layer in (0, 1):
            for what, chunks in (("in", CHUNKS[layer]), ("out", OUT_CHUNKS)):
                for c, (kind, _, w) in enumerate(chunks):
                    outs_before[layer, what, c] = o
                    o += NT if kind == "tok" else w // P
        PROJ_BANKS = 6

        def residual_ready(eng, n):
            layer, experts = divmod(n - 1, 2)
            if experts:
                eng.wait_ge(sem("comb_x"), 16 * (layer + 1))
            else:
                eng.wait_ge(sem("proj_ev"), outs_before[layer, "out", 2] + NT)

        unit_at = [(i, j) for i, (_, _, _, n) in enumerate(plan) for j in range(n)]

        def used_value(i, j):
            _, what, c, _ = plan[i]
            if what != "moe":
                return units_before[i] + j + 1
            if j < 2:
                return units_before[i - c] + (3 * c + j if c else j + 1)
            return units_before[i - c] + min(3 * c + 5, 3 * G * E)

        def chunk_done(eng, layer, what, c):
            eng.wait_ge(sem("unit_used"), unit_of[layer, what, c] + 4)

        @block.sync
        def _(sp):
            xv = x.rearrange("b (i p) d -> p (b i) d", p=P)
            sp.dma_start(X[:, :, :], xv).then_inc(sem("x_in"), 16)
            sp.dma_start(CT[:, :], consts).then_inc(sem("ct_in"), 16)
            w_in, w_out = (ev_w_in, od_w_in), (ev_w_out, od_w_out)
            def overflow(l):
                sp.wait_ge(sem("m_ovi"), l + 1)
                over = sp.value_load(OVI[0:1, l, 0:1], min_val=0, max_val=1)
                g = sp.value_load(OVI[0:1, l, 1:2], min_val=0, max_val=G - 1)
                with sp.If(over > 0):
                    with sp.Fori(0, E) as e:
                        sp.wait_ge(sem(f"ov{l}_dve"), 6 * e + 6)
                        for j, w in enumerate((moe_w_gate, moe_w_up)):
                            sp.dma_start(RAW[:, 0, j * D:(j + 1) * D],
                                         w[l].rearrange("g e (p k) f -> p (g e) (k f)", p=P)[:, bass.ds(g * E + e, 1), :]
                                         ).then_inc(sem(f"ov{l}_in"), 16)
                        sp.dma_start(RAW[:, 0, 2 * D:3 * D],
                                     moe_w_down[l].rearrange("g e p n -> p (g e) n")[:, bass.ds(g * E + e, 1), :]
                                     ).then_inc(sem(f"ov{l}_in"), 16)
                    sp.wait_ge(sem(f"ov{l}_dve"), OV_DVE)
                sp.end_ifs()

            for i, (layer, what, c, _) in enumerate(plan[:limit]):
                if i and plan[i - 1][1:3] == ("moe", G * E - 1):
                    overflow(plan[i - 1][0])
                if i >= SLOTS:
                    sp.wait_ge(sem("unit_lo"), units_before[i - SLOTS + 1])
                s = i % SLOTS
                landed = sem(f"landed{s}")
                if what == "moe":
                    g, e = divmod(c, E)
                    for j, w in enumerate((moe_w_gate, moe_w_up)):
                        sp.dma_start(RAW[:, s, j * D:(j + 1) * D],
                                     w[layer, g, e].rearrange("(p k) f -> p (k f)", p=P)).then_inc(landed, 16)
                    sp.dma_start(RAW[:, s, 2 * D:3 * D], moe_w_down[layer, g, e]).then_inc(landed, 16)
                else:
                    w = (w_in if what == "in" else w_out)[layer]
                    _, c0, n = (CHUNKS[layer] if what == "in" else OUT_CHUNKS)[c]
                    sp.dma_start(RAW[:, s, 0:KT * n].rearrange("p (k n) -> p k n", k=KT),
                                 w[0, :, c0:c0 + n].rearrange("(k p) n -> p k n", p=P)).then_inc(landed, 16)
            if stop == 2 or stop == 4:
                overflow(stop // 2 - 1)
            residual_ready(sp, stop)
            sp.dma_start(out.rearrange("b (i p) d -> p (b i) d", p=P), X[:, :, :]).then_inc(sem("out"), 16)
            sp.wait_ge(sem("out"), 16)

        landed_value = []
        tally = [0] * SLOTS
        for i, (_, what, _, _) in enumerate(plan):
            tally[i % SLOTS] += 48 if what == "moe" else 16
            landed_value.append(tally[i % SLOTS])

        def unit_views(i, j):
            layer, what, c, n = plan[i]
            s, u = i % SLOTS, (units_before[i] + j) % UNITS
            if what != "moe":
                w = (CHUNKS[layer] if what == "in" else OUT_CHUNKS)[c][2]
                return RAW[:, s, 2 * j * w:2 * (j + 1) * w], WH[:, u, 0:2 * w], WL[:, u, 0:2 * w]
            if j < 2:
                raw = RAW[:, s, 0:2 * D].rearrange("p (m k) -> p m k", m=2)[:, :, j * 512:(j + 1) * 512]
                return (raw, WH[:, u, :].rearrange("p (m k) -> p m k", m=2),
                        WL[:, u, :].rearrange("p (m k) -> p m k", m=2))
            return RAW[:, s, 2 * D:3 * D], WH[:, u, :], WL[:, u, :]

        def overflow_views(j):
            if j < 2:
                raw = RAW[:, 0, 0:2 * D].rearrange("p (m k) -> p m k", m=2)[:, :, j * 512:(j + 1) * 512]
                return (raw, *(w[:, j, :].rearrange("p (m k) -> p m k", m=2) for w in (WH, WL)))
            return RAW[:, 0, 2 * D:3 * D], WH[:, 2, :], WL[:, 2, :]

        def split_hi(act, i, j):
            u = units_before[i] + j
            if j == 0:
                act.wait_ge(sem(f"landed{i % SLOTS}"), landed_value[i])
            if u >= UNITS:
                act.wait_ge(sem("unit_used"), used_value(*unit_at[u - UNITS]))
            raw, hi, _ = unit_views(i, j)
            done(nc.scalar.activation(hi, raw, ACT.Copy), "unit_hi")

        def split_lo(dve, i, j):
            u = units_before[i] + j
            dve.wait_ge(sem("unit_hi"), u + 1)
            raw, hi, lo = unit_views(i, j)
            done(nc.vector.tensor_tensor(out=lo, in0=raw, in1=hi.bitcast(F32), op=ALU.subtract), "unit_lo")

        def product(ps, ah, al, bh, bl, start, stop):
            nc.tensor.matmul(ps, ah, bh, start=start, stop=False)
            nc.tensor.matmul(ps, ah, bl, start=False, stop=False)
            return nc.tensor.matmul(ps, al, bh, start=False, stop=stop)

        def project(pe, layer, what, c, lhs_ready):
            kind, _, w = (CHUNKS[layer] if what == "in" else OUT_CHUNKS)[c]
            i = slot_of[layer, what, c]
            o = outs_before[layer, what, c]
            n_out = NT if kind == "tok" else w // P
            if o + n_out > PROJ_BANKS:
                pe.wait_ge(sem("proj_ev"), o + n_out - PROJ_BANKS)
            for j in range(4):
                u = units_before[i] + j
                pe.wait_ge(sem("unit_lo"), u + 1)
                wh = WH[:, u % UNITS, 0:2 * w].rearrange("p (k n) -> p k n", k=2)
                wl = WL[:, u % UNITS, 0:2 * w].rearrange("p (k n) -> p k n", k=2)
                for kk in range(2):
                    k = 2 * j + kk
                    if lhs_ready is not None:
                        pe.wait_ge(sem("hT_lo"), lhs_ready + k // 2 + 1)
                    for n in range(n_out):
                        bank = (o + n) % PROJ_BANKS
                        if kind == "tok":
                            ts = slice(n * P, (n + 1) * P)
                            last = product(PS[:, bank, 0:w], HTH[:, k, ts], HTL[:, k, ts], wh[:, kk, :], wl[:, kk, :],
                                           k == 0, k == KT - 1)
                        else:
                            cs = slice(n * P, (n + 1) * P)
                            nc.tensor.matmul(PS[:, bank, 0:T], wh[:, kk, cs], HTH[:, k, :], start=k == 0, stop=False)
                            nc.tensor.matmul(PS[:, bank, 0:T], wh[:, kk, cs], HTL[:, k, :], start=False, stop=False)
                            last = nc.tensor.matmul(PS[:, bank, 0:T], wl[:, kk, cs], HTH[:, k, :], start=False,
                                                    stop=k == KT - 1)
                done(last, "unit_used")


        mw_at = [0]

        def mw(n):
            a = mw_at[0]
            mw_at[0] += n
            return MW[:, a:a + n]

        MGL, MEL, MMX, MEX, MR1, MR2 = mw(8), mw(64), mw(10), mw(72), mw(512), mw(512)
        MOH, MSE_, MSU, MGT, MKY = mw(8), mw(64), mw(10), mw(64), mw(8)
        MOV, MOF, MIN_, MGO, MPO, MKO = mw(4), mw(2), mw(8), mw(16), mw(8), mw(2)

        sm_at = [0]

        def sm(n):
            a = sm_at[0]
            sm_at[0] += n
            assert sm_at[0] <= 512
            return SM[:, a:a + n]

        def bc(ap, axis, shape):
            return ap.unsqueeze(axis).to_broadcast(shape)

        NH, MS, MSE, RS = sm(64), sm(2), sm(2), sm(2)
        ASS, ARS, AMX, ASM, ADEN = sm(20), sm(20), sm(16), sm(16), sm(16)
        LBM, LBE, LBS, LBC, LBO, LBH, LBN, BL01 = sm(4), sm(12), sm(4), sm(4), sm(4), sm(4), sm(4), sm(4)
        BSS, BRS = sm(8), sm(8)
        BT2, XA, XB_, XE, GL, EA, BCOL, CSS, CRK, BH = (sm(16), sm(16), sm(16), sm(16), sm(16), sm(8), sm(24),
                                                        sm(32), sm(32), sm(16))
        COS_, DMU, DSS, DRS = sm(16), sm(8), sm(8), sm(8)
        RBV = at("RBV", [P, NT, 24], arena - size([P, D]))

        RKT = at("RKT", [8, 3, T], arena - size([P, D]) + 256)

        def rsqrt(pool, link, name, out, ss, tmp, scale, n=1, rows=slice(0, P)):
            width = ss.shape[1]
            link(nc.gpsimd.tensor_scalar(out=tmp, in0=ss, scalar1=scale, scalar2=EPS, op0=ALU.mult, op1=ALU.add))
            done(nc.gpsimd.tensor_tensor(out=out, in0=tmp, in1=NH[:, 0:width], op=ALU.pow), name)

        proj_total = {0: outs_before[0, "out", 0], 1: outs_before[1, "out", 0]}
        N_PAR = 13

        @block.gpsimd
        def _(pool):
            link = linker(pool, "pool_step")
            link(nc.gpsimd.memset(NH, -0.5))
            n_par = 0

            def param(dst, src):
                pool.dma_start(dst, src).then_inc(sem("par_in"), 16)
                return 1

            def gain(n, src):
                if n:
                    pool.wait_ge(sem("h"), n)
                if n == 3:
                    pool.wait_ge(sem("c_kb"), 1)
                pool.dma_start(GB[:, :], src.partition_broadcast(P)).then_inc(sem("gb_in"), 16)

            gain(0, mix_norm[0])
            link(nc.gpsimd.memset(ROWS[:, :], 0.0))
            n_par += param(ROWS[0:48, :], c_conv_w[0].rearrange("j (b p) -> (j b) p", p=P))
            n_par += param(ROWS[48:60, :], b_lb_logits.rearrange("l (h p) -> (l h) p", p=P))
            for r, w in ((60, a_q_gain), (61, a_k_gain)):
                n_par += param(ROWS[r:r + 1, 0:64], w)
                n_par += param(ROWS[r:r + 1, 64:128], w)
            pool.dma_start(MKF[:, :, :], masks).then_inc(sem("mk_in"), 16)
            n_par += param(SINK, a_sinks[0].partition_broadcast(P))
            n_par += param(BGAIN, b_out_gain[0].partition_broadcast(P))
            n_par += param(CGAIN, c_out_gain[0].partition_broadcast(P))
            n_par += param(ALOG, c_a_log[0].partition_broadcast(P))
            n_par += param(DTB, c_dt_bias[0].partition_broadcast(P))
            n_par += param(RB[:, :, 0:G], moe_b_rg.rearrange("(o l) n -> o l n", o=1).to_broadcast([P, 2, G]))
            n_par += param(RB[:, :, G:], moe_b_re.rearrange("(o l) n -> o l n", o=1).to_broadcast([P, 2, G * E]))
            for l in range(2):
                pool.dma_start(RW[:, l, :, 0:G], moe_w_rg[l].rearrange("(p k) n -> p k n", p=P)).then_inc(sem("rw_in"), 16)
                pool.dma_start(RW[:, l, :, G:], moe_w_re[l].rearrange("(p k) n -> p k n", p=P)).then_inc(sem("rw_in"), 16)
            assert n_par == N_PAR

            def norm(n):
                pool.wait_ge(sem("ms"), 2 * n + 2)
                rsqrt(pool, link, "rs", RS, MS, MSE, 1.0)

            pool.wait_ge(sem("mk_in"), 16)
            done(nc.gpsimd.tensor_copy(MK[:, :, :], MKF[:, :, :]), "mask")
            norm(0)
            chunk_done(pool, 0, "in", len(CHUNKS[0]) - 1)
            link(nc.gpsimd.memset(RST[:, :], 1.0))
            done(nc.gpsimd.memset(RST[:, :].rearrange("p (c t) -> p c t", t=CH)[:, :, 0:1], 0.0), "b_rst")
            done(nc.gpsimd.memset(SB[0:64, 0, :, 64:128], NEG), "a_pad")
            pool.wait_ge(sem("sumsq"), 1)
            rsqrt(pool, link, "root", ARS, ASS, ASS, 1.0 / 64)
            pool.wait_ge(sem("b_scan"), 1)
            bf = LB[:, :, :].rearrange("p h t -> p (h t)")
            for L in range(1, 9):
                if L >= 3:
                    pool.wait_ge(sem("b_ml"), L - 2)
                d = DL[:, L % 2, :]
                if L <= 6:
                    h = 2 ** (L - 1)
                    v = bf.rearrange("p (n c) -> p n c", c=2 * h)
                    dv = d.rearrange("p (n c) -> p n c", c=2 * h)
                    n = v.shape[1]
                    ref = v[:, :, h - 1:h].to_broadcast([P, n, h])
                    done(nc.gpsimd.tensor_tensor(out=dv[:, :, h:], in0=v[:, :, h:], in1=ref, op=ALU.subtract), "b_d")
                    done(nc.gpsimd.tensor_tensor(out=dv[:, :, 0:h], in0=ref, in1=v[:, :, 0:h], op=ALU.subtract), "b_d")
                elif L == 7:
                    v, dv = (a.rearrange("p (n c) -> p n c", c=P) for a in (bf, d))
                    done(nc.gpsimd.tensor_copy(dv[:, :, CH:], v[:, :, CH:]), "b_d")
                    done(nc.gpsimd.tensor_tensor(out=dv[:, :, 0:CH], in0=v[:, :, CH - 1:CH].to_broadcast([P, 8, CH]),
                                                 in1=v[:, :, 0:CH], op=ALU.subtract), "b_d")
                else:
                    v, dv = LB[:, :, :], d.rearrange("p (h t) -> p h t", h=4)
                    sh = [P, 4, CH]
                    bl = BL01.unsqueeze(2)
                    link(nc.gpsimd.tensor_tensor(out=bl, in0=v[:, :, 63:64], in1=v[:, :, 127:128], op=ALU.add))
                    nc.gpsimd.tensor_copy(dv[:, :, 128:192], v[:, :, 128:192])
                    nc.gpsimd.tensor_tensor(out=dv[:, :, 192:256], in0=v[:, :, 192:256],
                                            in1=v[:, :, 191:192].to_broadcast(sh), op=ALU.add)
                    done(nc.gpsimd.tensor_tensor(out=dv[:, :, 64:128], in0=v[:, :, 127:128].to_broadcast(sh),
                                                 in1=v[:, :, 64:128], op=ALU.subtract), "b_d")
                    done(nc.gpsimd.tensor_tensor(out=dv[:, :, 0:64], in0=bl.to_broadcast(sh),
                                                 in1=v[:, :, 0:64], op=ALU.subtract), "b_d")
            pool.wait_ge(sem("sumsq"), 2)
            rsqrt(pool, link, "root", BRS, BSS, BSS, 1.0 / 128)
            if stop == 1:
                return
            gain(1, moe_norm[0])
            norm(1)
            if stop == 2:
                return
            gain(2, mix_norm[1])
            norm(2)
            residual_ready(pool, 2)
            pool.wait_ge(sem("h"), 3)
            done(nc.gpsimd.memset(CB[:, :, 0:3], 0.0), "c_pad")
            pool.dma_start(DG[:, :], d_out_gain.rearrange("o h n -> o (h n)")[0].partition_broadcast(P)).then_inc(sem("dg_in"), 16)
            pool.dma_start(DB[:, :], d_out_bias.rearrange("o h n -> o (h n)")[0].partition_broadcast(P)).then_inc(sem("dg_in"), 16)
            chunk_done(pool, 1, "in", len(CHUNKS[1]) - 1)
            pool.wait_ge(sem("proj_ev"), proj_total[1])
            xr = TM[:, :, 528:1040].rearrange("p i (h n) -> p i h n", n=64)
            x1, x2 = xr[:, :, :, 0:32], xr[:, :, :, 32:64]
            cos, sin = (CT[:, c:c + 64].rearrange("p (i n) -> p i n", i=2).unsqueeze(2).to_broadcast([P, 2, 8, 32])
                        for c in (C_COS, C_SIN))
            r1, r2 = QRD[:, :, :, 0:32], QRD[:, :, :, 32:64]
            t1, t2 = TMP[:, :, :, 0:32], TMP[:, :, :, 32:64]
            for i in range(NT):
                nc.gpsimd.tensor_tensor(out=r1[:, i], in0=x1[:, i], in1=cos[:, i], op=ALU.mult)
                nc.gpsimd.tensor_tensor(out=r2[:, i], in0=x1[:, i], in1=sin[:, i], op=ALU.mult)
                nc.gpsimd.tensor_tensor(out=t1[:, i], in0=x2[:, i], in1=sin[:, i], op=ALU.mult)
                link(nc.gpsimd.tensor_tensor(out=t2[:, i], in0=x2[:, i], in1=cos[:, i], op=ALU.mult))
                done(nc.gpsimd.tensor_tensor(out=r1[:, i], in0=r1[:, i], in1=t1[:, i], op=ALU.subtract), "d_rot")
                done(nc.gpsimd.tensor_tensor(out=r2[:, i], in0=r2[:, i], in1=t2[:, i], op=ALU.add), "d_rot")
            pool.wait_ge(sem("sumsq"), 3)
            done(nc.gpsimd.tensor_tensor(out=CRK, in0=CSS, in1=NH[:, 0:32], op=ALU.pow), "root")
            pool.wait_ge(sem("sumsq"), 4)
            rsqrt(pool, link, "root", DRS, DSS, DSS, 1.0 / 128)
            pool.wait_ge(sem("sumsq"), 5)
            rsqrt(pool, link, "root", COS_, COS_, COS_, 1.0 / 64)
            if stop == 3:
                return
            gain(3, moe_norm[1])
            norm(3)

        @block.scalar
        def _(act):
            link = linker(act, "act_step")

            def norm(n):
                if n == 0:
                    act.wait_ge(sem("x_in"), 16)
                else:
                    residual_ready(act, n)
                for i in range(NT):
                    done(nc.scalar.activation(H[:, i, :], X[:, i, :], ACT.Square, scale=1.0 / 32,
                                              accum_out=MS[:, i:i + 1]), "ms")

            def lhs_hi(n):
                for b in range(4):
                    act.wait_ge(sem("hT_ps"), 4 * n + b + 1)
                    done(nc.scalar.activation(HTH[:, 2 * b:2 * b + 2, :], PS[:, b, :].rearrange("p (k t) -> p k t", k=2),
                                              ACT.Copy), "hT_hi")

            def evacuate(layer, c):
                kind, c0, w = CHUNKS[layer][c]
                o = outs_before[layer, "in", c]
                for n in range(NT if kind == "tok" else w // P):
                    chunk_done(act, layer, "in", c)
                    ps = PS[:, (o + n) % PROJ_BANKS, :]
                    if kind == "tok":
                        dst = (TM[:, n, c0 - 1536:c0 - 1536 + w] if layer else
                               TA[:, n, c0:c0 + w] if c0 < 768 else TB[:, n, c0 - 1792:c0 - 1792 + w])
                        done(nc.scalar.activation(dst, ps[:, 0:w], ACT.Copy), "proj_ev")
                    elif layer:
                        done(nc.scalar.activation(CB[:, 3 * c + n, 3:3 + T], ps[:, 0:T], ACT.Copy), "proj_ev")
                    else:
                        blk = (c0 - 768) // P + n
                        if blk < 4:
                            nc.scalar.activation(TQ[:, blk, :], ps[:, 0:T], ACT.Tanh, scale=0.5)
                            done(nc.scalar.activation(QR[:, blk, :], ps[:, 0:T], ACT.Copy), "proj_ev")
                        else:
                            done(nc.scalar.activation(TF[:, blk - 4, :], ps[:, 0:T], ACT.Tanh, scale=0.5), "proj_ev")

            def in_projection(layer, between=lambda c: None):
                n = len(CHUNKS[layer])
                for c in range(n):
                    i = slot_of[layer, "in", c]
                    for j in range(3):
                        split_hi(act, i, j)
                    if c == 0:
                        lhs_hi(2 * layer)
                    else:
                        evacuate(layer, c - 1)
                    split_hi(act, i, 3)
                    between(c)
                evacuate(layer, n - 1)

            def out_projection(layer):
                act.wait_ge(sem("mix"), layer + 1)
                for c in range(3):
                    for j in range(4):
                        split_hi(act, slot_of[layer, "out", c], j)
                    if c == 0:
                        lhs_hi(2 * layer + 1)

            def moe(l):
                for b in range(4):
                    act.wait_ge(sem("m_T"), 4 * l + b + 1)
                    done(nc.scalar.activation(HTF[:, 2 * b:2 * b + 2, :], PS[:, b, :].rearrange("p (k t) -> p k t", k=2),
                                              ACT.Copy), "m_ht")
                act.wait_ge(sem("h"), 2 * l + 2)
                done(nc.scalar.activation(HH[:, :, :], H[:, :, :], ACT.Copy), "m_hh")
                act.wait_ge(sem("m_ld"), l + 1)
                done(nc.scalar.activation(MEX, MEX, ACT.Exp), "m_ex")
                act.wait_ge(sem("m_pf"), 2 * l + 2)
                done(nc.scalar.activation(PR[:, :, :, :], PF[:, :, :, :], ACT.Copy), "m_pr")
                act.wait_ge(sem("m_pt"), l + 1)
                done(nc.scalar.activation(PTR[:, :, :], PS[:, 1:3, :].rearrange("p a (g t) -> p (a g) t", t=T), ACT.Copy),
                     "m_ptr")

                def gather_hi(g):
                    for b in range(2):
                        act.wait_ge(sem("g_ps"), 8 * l + 2 * g + b + 1)
                        done(nc.scalar.activation(GTH[:, g % 2, 4 * b:4 * b + 4, :],
                                                  PS[:, 5 + b, :].rearrange("p (k j) -> p k j", k=4), ACT.Copy), "g_hi")

                def silu(n):
                    act.wait_ge(sem("unit_used"), used_value(slot_of[l, "moe", n], 1))
                    if n >= 2:
                        act.wait_ge(sem("hid"), 32 * l + n - 1)
                    done(nc.scalar.activation(SIL[:, n % 2, :], PS[:, n % 2, 0:P], ACT.Silu), "silu")

                def hid_hi(n):
                    act.wait_ge(sem("hid_T"), 32 * l + n + 1)
                    if n >= 2:
                        act.wait_ge(sem("unit_used"), used_value(slot_of[l, "moe", n - 2], 2))
                    done(nc.scalar.activation(HIH[:, n % 2, :], PS[:, 2, (n % 2) * P:(n % 2) * P + P], ACT.Copy), "hid_hi")

                def y_out(g):
                    act.wait_ge(sem("unit_used"), used_value(slot_of[l, "moe", 8 * g + 7], 2))
                    if g or l:
                        act.wait_ge(sem("comb"), 4 * (4 * l + g))
                    done(nc.scalar.activation(YS[:, :], PS[:, 3:5, :].rearrange("p a n -> p (a n)"), ACT.Copy), "y_sb")

                gather_hi(0)
                for n in range(G * E + 1):
                    if n:
                        silu(n - 1)
                    if n < G * E:
                        for j in range(3):
                            split_hi(act, slot_of[l, "moe", n], j)
                        if n % E == 6 and n // E < G - 1:
                            gather_hi(n // E + 1)
                    if n:
                        hid_hi(n - 1)
                        if n % E == 0:
                            y_out(n // E - 1)
                overflow(l)

            def overflow(l):
                act.wait_ge(sem("m_ovi"), l + 1)
                over = act.value_load(OVI[0:1, l, 0:1], min_val=0, max_val=1)
                with act.If(over > 0):
                    act.wait_ge(sem("comb_x"), 16 * (l + 1))
                    act.wait_ge(sem(f"ov{l}_dve"), 2)
                    done(nc.scalar.activation(PR[:, :, 0, :], PF[:, :, 0, :], ACT.Copy), f"ov{l}_act")
                    act.wait_ge(sem(f"ov{l}_pe"), 1)
                    done(nc.scalar.activation(PTR[:, 0, :], PS[:, 1, 0:T], ACT.Copy), f"ov{l}_act")
                    for b in range(2):
                        act.wait_ge(sem(f"ov{l}_pe"), 3 + b)
                        done(nc.scalar.activation(GTH[:, 0, 4 * b:4 * b + 4, :],
                                                  PS[:, 5 + b, :].rearrange("p (k j) -> p k j", k=4), ACT.Copy), f"ov{l}_act")
                    with act.Fori(0, E) as e:
                        act.wait_ge(sem(f"ov{l}_in"), 48 * e + 48)
                        for j in range(3):
                            raw, hi = overflow_views(j)[:2]
                            done(nc.scalar.activation(hi, raw, ACT.Copy), f"ov{l}_act")
                        act.wait_ge(sem(f"ov{l}_pe"), 3 * e + 5)
                        done(nc.scalar.activation(SIL[:, 0, :], PS[:, 0, 0:P], ACT.Silu), f"ov{l}_act")
                        act.wait_ge(sem(f"ov{l}_pe"), 3 * e + 6)
                        done(nc.scalar.activation(HIH[:, 0, :], PS[:, 2, 0:P], ACT.Copy), f"ov{l}_act")
                    act.wait_ge(sem(f"ov{l}_dve"), OV_DVE)
                act.end_ifs()

            act.wait_ge(sem("pt_ps"), 1)
            done(nc.scalar.activation(PT[:, 0:62], PS[:, 7, 0:62], ACT.Copy), "pt")
            norm(0)
            act.wait_ge(sem("mask"), 1)
            act.wait_ge(sem("lb_d"), 1)
            done(nc.scalar.activation(LBE, LBE, ACT.Exp), "lb_e")
            in_projection(0)
            chunk_done(act, 0, "in", len(CHUNKS[0]) - 1)
            act.wait_ge(sem("hT_lo"), 4)
            act.wait_ge(sem("proj_ev"), proj_total[0])
            done(nc.scalar.activation(TG[:, :, :], TB[:, :, 512:], ACT.Tanh, scale=0.5), "b_tg")
            act.wait_ge(sem("lb"), 1)
            for h in range(4):
                done(nc.scalar.activation(LB[:, h, :], TF[:, h, :], ACT.Ln, scale=LBC[:, h:h + 1], bias=LBO[:, h:h + 1]), "b_ln")
            for n in range(3):
                act.wait_ge(sem("a_T"), n + 1)
                dst = QT[:, 2 * n:2 * n + 2, :] if n < 2 else KTT[:, :, :]
                done(nc.scalar.activation(dst, PS[:, n, :].rearrange("p (a t) -> p a t", a=2), ACT.Copy,
                                          scale=PT[:, 60 + n // 2:61 + n // 2]), "a_QT")

            def b_exp(L):
                act.wait_ge(sem("b_d"), 2 * L)
                done(nc.scalar.activation(DL[:, L % 2, :], DL[:, L % 2, :], ACT.Exp), "b_e")

            b_exp(1)
            act.wait_ge(sem("a_pad"), 1)
            act.wait_ge(sem("a_S"), 1)
            nc.scalar.activation(SB[0:64, 0, :, 0:64], PS[0:64, 0:2, :].rearrange("p a (h k) -> p (a h) k", k=P)[:, :, 0:64],
                                 ACT.Copy, scale=0.125)
            done(nc.scalar.activation(SB[64:128, 0, :, :], PS[64:128, 0:2, :].rearrange("p a (h k) -> p (a h) k", k=P),
                                      ACT.Copy, scale=0.125), "a_SB")
            act.wait_ge(sem("a_S"), 2)
            done(nc.scalar.activation(SB[:, 1, :, :], PS[:, 2:4, :].rearrange("p a (h k) -> p (a h) k", k=P),
                                      ACT.Copy, scale=0.125), "a_SB")
            b_exp(2)
            b_exp(3)
            for i in range(NT):
                act.wait_ge(sem("a_D"), i + 1)
                done(nc.scalar.activation(SB[:, i, :, :], SB[:, i, :, :], ACT.Exp), "a_P")
            done(nc.scalar.activation(ASM, ASM, ACT.Exp), "a_es")
            b_exp(4)
            for n in range(4):
                act.wait_ge(sem("a_PT"), n + 1)
                done(nc.scalar.activation(PTS[:, n // 2, 4 * (n % 2):4 * (n % 2) + 4, :],
                                          PS[:, n, :].rearrange("p (h t) -> p h t", h=4), ACT.Copy), "a_PTS")
            for L in range(5, 9):
                b_exp(L)
            act.wait_ge(sem("b_cp"), 7)
            act.wait_ge(sem("b_mm"), 8)
            done(nc.scalar.activation(AT[0:64, :, :, CH:].rearrange("p i h t -> p (i h) t"),
                                      PS[0:64, 6, :].rearrange("p (n t) -> p n t", n=8), ACT.Copy), "b_off")
            act.wait_ge(sem("b_mm"), 9)
            done(nc.scalar.activation(AXB[:, :, :], PS[:, 4, :].rearrange("p (h t) -> p h t", h=4), ACT.Copy), "b_off")
            act.wait_ge(sem("b_O"), 2)
            done(nc.scalar.activation(SQB[:, :, :, :], PS[:, 6:8, :].rearrange("p i (h n) -> p i h n", h=4), ACT.Square), "b_sq")
            out_projection(0)
            if stop == 1:
                return
            norm(1)
            moe(0)
            if stop == 2:
                return
            norm(2)

            def conv_tanh(c):
                act.wait_ge(sem("c_conv"), 3 * c + 3)
                done(nc.scalar.activation(CB[:, 3 * c:3 * c + 3, 0:T], SL[:, 3 * c:3 * c + 3, :], ACT.Tanh, scale=0.5), "c_tanh")

            act.wait_ge(sem("c_pad"), 1)
            in_projection(1, lambda c: conv_tanh(c - 2) if 2 <= c < 6 else None)
            act.wait_ge(sem("c_silu"), 4)
            done(nc.scalar.activation(SQC[:, :, :], SL[:, 0:8, :], ACT.Square), "c_sqc")
            act.wait_ge(sem("proj_ev"), proj_total[1])
            done(nc.scalar.activation(BT2.rearrange("p (i h) -> p i h", i=2), TM[:, :, 512:520], ACT.Tanh, scale=0.5), "c_bt")
            chunk_done(act, 1, "in", len(CHUNKS[1]) - 1)
            act.wait_ge(sem("hT_lo"), 12)
            done(nc.scalar.activation(SG[:, :, :], TM[:, :, 0:512], ACT.Tanh, scale=0.5), "c_tz")
            act.wait_ge(sem("c_xa"), 2)
            link(nc.scalar.activation(XE, XB_, ACT.Exp, scale=-1.0))
            done(nc.scalar.activation(XE, XE, ACT.Ln, bias=1.0), "c_sp")
            done(nc.scalar.activation(EA, ALOG, ACT.Exp), "c_ea")
            act.wait_ge(sem("d_rot"), 4)
            done(nc.scalar.activation(TMP[:, :, :, :].rearrange("p i h n -> p i (h n)"), TM[:, :, 1552:2064], ACT.Tanh, scale=0.5), "d_tg")
            for b in range(2):
                act.wait_ge(sem("d_T"), b + 1)
                done(nc.scalar.activation(QTD[:, 2 * b:2 * b + 2, :], PS[:, b, :].rearrange("p (a t) -> p a t", a=2), ACT.Copy), "d_QT")
            act.wait_ge(sem("c_rT"), 1)
            done(nc.scalar.activation(RKT[:, :, :], PS[0:8, 0:2, :].rearrange("p a (b t) -> p (a b) t", t=T)[:, 0:3, :],
                                      ACT.Copy), "c_rkt")
            act.wait_ge(sem("c_ga"), 3)
            done(nc.scalar.activation(GA[:, :, :], GA[:, :, :], ACT.Exp), "c_gexp")
            act.wait_ge(sem("d_xc"), 1)
            done(nc.scalar.activation(SQD[:, :, :], QRD[:, :, :, :].rearrange("p i h n -> p i (h n)"), ACT.Square), "d_sq")
            for gr in range(4):
                act.wait_ge(sem("c_T"), gr + 1)
                done(nc.scalar.activation(XI[:, gr // 2, 4 * (gr % 2):4 * (gr % 2) + 4, :],
                                          PS[:, 2 * gr, :].rearrange("p (h t) -> p h t", h=4), ACT.Copy), "c_X")
            for L in range(1, 7):
                for gr in range(4):
                    act.wait_ge(sem("c_Q"), 4 * (L - 1) + gr + 1)
                    done(nc.scalar.activation(QI[:, gr // 2, 4 * (gr % 2):4 * (gr % 2) + 4, :],
                                              PS[:, 2 * gr, :].rearrange("p (h t) -> p h t", h=4), ACT.Copy), "c_Qs")
                if L < 6:
                    for gr in range(4):
                        act.wait_ge(sem("c_T"), 4 * L + gr + 1)
                        done(nc.scalar.activation(XI[:, gr // 2, 4 * (gr % 2):4 * (gr % 2) + 4, :],
                                                  PS[:, 2 * gr, :].rearrange("p (h t) -> p h t", h=4), ACT.Copy), "c_X")
            for i in range(NT):
                act.wait_ge(sem("c_U"), i + 1)
                done(nc.scalar.activation(U[:, i, :, :], PS[:, 2 * i, :].rearrange("p (h n) -> p h n", h=8), ACT.Copy), "c_Us")
            act.wait_ge(sem("c_O"), 2)
            done(nc.scalar.activation(SQC[:, 0:4, :].rearrange("p a n -> p (a n)").rearrange("p (i n) -> p i n", i=2),
                                      PS[:, 3:5, :], ACT.Square), "c_osq")
            out_projection(1)
            if stop == 3:
                return
            norm(3)
            moe(1)

        @block.vector
        def _(dve):
            link = linker(dve, "dve_step")

            def tt(out, a, b, op):
                return nc.vector.tensor_tensor(out=out, in0=a, in1=b, op=op)

            def ts(out, a, s1, op0, s2=None, op1=None):
                if op1 is None:
                    return nc.vector.tensor_scalar(out=out, in0=a, scalar1=s1, scalar2=None, op0=op0)
                return nc.vector.tensor_scalar(out=out, in0=a, scalar1=s1, scalar2=s2, op0=op0, op1=op1)

            def stt(out, a, s, b, op0, op1):
                return nc.vector.scalar_tensor_tensor(out=out, in0=a, scalar=s, in1=b, op0=op0, op1=op1)

            def total(out, a, op=ALU.add):
                return nc.vector.tensor_reduce(out=out, in_=a, axis=AX, op=op)

            MUL, ADD, SUB = ALU.mult, ALU.add, ALU.subtract

            def norm(n):
                dve.wait_ge(sem("gb_in"), 16 * (n + 1))
                dve.wait_ge(sem("rs"), n + 1)
                for i in range(NT):
                    ins = stt(H[:, i, :], X[:, i, :], RS[:, i:i + 1], GB[:, :], MUL, MUL)
                    if i:
                        done(ins, "h")

            def lhs_lo(n):
                for b in range(4):
                    dve.wait_ge(sem("hT_hi"), 4 * n + b + 1)
                    done(tt(HTL[:, 2 * b:2 * b + 2, :], PS[:, b, :].rearrange("p (k t) -> p k t", k=2),
                            HTH[:, 2 * b:2 * b + 2, :].bitcast(F32), SUB), "hT_lo")

            def in_projection(layer, between=lambda c: None):
                for c in range(len(CHUNKS[layer])):
                    for j in range(3):
                        split_lo(dve, slot_of[layer, "in", c], j)
                    if c == 0:
                        lhs_lo(2 * layer)
                    split_lo(dve, slot_of[layer, "in", c], 3)
                    between(c)

            def out_projection(layer):
                def add(c):
                    _, c0, w = OUT_CHUNKS[c]
                    for n in range(NT):
                        o = outs_before[layer, "out", c] + n
                        chunk_done(dve, layer, "out", c)
                        ins = tt(X[:, n, c0:c0 + w], PS[:, o % PROJ_BANKS, 0:w], X[:, n, c0:c0 + w], ADD)
                        done(ins, "proj_ev")
                dve.wait_ge(sem("mix"), layer + 1)
                for c in range(3):
                    for j in range(4):
                        split_lo(dve, slot_of[layer, "out", c], j)
                    if c == 0:
                        lhs_lo(2 * layer + 1)
                    else:
                        add(c - 1)
                add(2)

            def moe(l):
                dve.wait_ge(sem("m_hh"), l + 1)
                done(tt(HL[:, :, :], H[:, :, :], HH[:, :, :].bitcast(F32), SUB), "m_hl")
                dve.wait_ge(sem("m_lg"), l + 1)
                lg = PS[:, 4, 0:72].rearrange("p (i n) -> p i n", i=2)
                link(tt(MGL.rearrange("p (i n) -> p i n", i=2), lg[:, :, 0:G], bc(RB[:, l, 0:G], 1, [P, 2, G]), ADD))
                link(tt(MEL.rearrange("p (i n) -> p i n", i=2), lg[:, :, G:], bc(RB[:, l, G:], 1, [P, 2, G * E]), ADD))
                gl = MGL.rearrange("p (i g) -> p i g", i=2)
                el = MEL.rearrange("p (n e) -> p n e", e=E)
                link(total(MMX[:, 0:2], gl, ALU.max))
                link(total(MMX[:, 2:10], el, ALU.max))
                link(tt(MEX[:, 0:8].rearrange("p (i g) -> p i g", i=2), gl, bc(MMX[:, 0:2], 2, [P, 2, G]), SUB))
                done(tt(MEX[:, 8:72].rearrange("p (n e) -> p n e", e=E), el, bc(MMX[:, 2:10], 2, [P, 8, E]), SUB), "m_ld")
                for vals, n, k, low, most, out in ((gl, 2, G, C_LOW4, 0.5, MOH), (el, 8, E, C_LOW8, 1.5, MSE_)):
                    sh = [P, n, k, k]
                    a = MR1[:, 0:n * k * k].rearrange("p (n a b) -> p n a b", n=n, a=k)
                    b = MR2[:, 0:n * k * k].rearrange("p (n a b) -> p n a b", n=n, a=k)
                    other, own = bc(vals, 2, sh), bc(vals, 3, sh)
                    lowc = bc(CT[:, low:low + k * k].rearrange("p (a b) -> p a b", a=k), 1, sh)
                    link(tt(a, other, own, ALU.is_gt))
                    link(tt(b, other, own, ALU.is_equal))
                    link(tt(b, b, lowc, MUL))
                    link(tt(a, a, b, ADD))
                    link(total(out, a.rearrange("p n a b -> p (n a) b")))
                    link(ts(out, out, most, ALU.is_lt), also="m_rank")
                dve.wait_ge(sem("m_ex"), l + 1)
                ex = MEX[:, 8:72].rearrange("p (n e) -> p n e", e=E)
                link(total(MSU[:, 0:2], MEX[:, 0:8].rearrange("p (i g) -> p i g", i=2)))
                link(tt(MEX[:, 8:72], MEX[:, 8:72], MSE_, MUL))
                link(total(MSU[:, 2:10], ex))
                link(nc.vector.reciprocal(MSU, MSU))
                w3 = MSU[:, 2:10].rearrange("p (i g) -> p i g", i=2)
                link(tt(w3, w3, bc(MSU[:, 0:2], 2, [P, 2, G]), MUL))
                link(tt(MSU[:, 2:10], MSU[:, 2:10], MOH, MUL))
                link(tt(MGT.rearrange("p (n e) -> p n e", e=E), ex, bc(MSU[:, 2:10], 2, [P, 8, E]), MUL), also="m_gate")
                dve.wait_ge(sem("m_pos"), l + 1)
                link(ts(MKY, MOH, -1e6, MUL, 1e6, ADD))
                link(nc.vector.tensor_copy(MPO, PS[:, 5, 0:8]))
                link(tt(MKY, MKY, MPO, ADD))
                link(ts(MOV, PS[:, 5, 8:12], float(P), ALU.is_gt))
                for i in range(NT):
                    done(tt(PF[:, i, :, :], bc(CT[:, C_IOTA:C_IOTA + P], 1, [P, G, P]),
                            bc(MKY[:, 4 * i:4 * i + 4], 2, [P, G, P]), ALU.is_equal), "m_pf")
                link(total(MOF[:, 0:1], MOV))
                link(tt(MIN_[:, 0:4], MOV, CT[:, C_IOTA:C_IOTA + G], MUL))
                link(total(MOF[:, 1:2], MIN_[:, 0:4]))
                done(nc.vector.tensor_copy(OVI[:, l, :], MOF), "m_ovi")
                dve.wait_ge(sem("m_gg"), l + 1)
                done(nc.vector.tensor_copy(GG[:, :], PS[:, 4, 0:G * E]), "m_ggs")

                def gather_lo(g):
                    for b in range(2):
                        dve.wait_ge(sem("g_hi"), 8 * l + 2 * g + b + 1)
                        done(tt(GTL[:, g % 2, 4 * b:4 * b + 4, :], PS[:, 5 + b, :].rearrange("p (k j) -> p k j", k=4),
                                GTH[:, g % 2, 4 * b:4 * b + 4, :].bitcast(F32), SUB), "g_lo")

                def hidden(n):
                    dve.wait_ge(sem("silu"), 32 * l + n + 1)
                    if n == 0:
                        dve.wait_ge(sem("m_ggs"), l + 1)
                    if n >= 2:
                        dve.wait_ge(sem("hid_T"), 32 * l + n - 1)
                    done(stt(HID[:, n % 2, :], SIL[:, n % 2, :], GG[:, n:n + 1], PS[:, n % 2, P:2 * P], MUL, MUL), "hid")

                def hid_lo(n):
                    dve.wait_ge(sem("hid_hi"), 32 * l + n + 1)
                    done(tt(HIL[:, n % 2, :], PS[:, 2, (n % 2) * P:(n % 2) * P + P], HIH[:, n % 2, :].bitcast(F32), SUB), "hid_lo")

                def combine(g):
                    for i in range(NT):
                        for b in range(2):
                            dve.wait_ge(sem("comb"), 4 * (4 * l + g) + 2 * i + b + 1)
                            xs = X[:, i, 512 * b:512 * b + 512]
                            ins = tt(xs, PS[:, 7, :], xs, ADD)
                            done(ins, "comb_x")

                gather_lo(0)
                for n in range(G * E + 1):
                    if n:
                        hidden(n - 1)
                    if n < G * E:
                        for j in range(3):
                            split_lo(dve, slot_of[l, "moe", n], j)
                        if n % E == 6 and n // E < G - 1:
                            gather_lo(n // E + 1)
                    if n:
                        hid_lo(n - 1)
                    if n >= E and (n % E == 1):
                        combine(n // E - 1)
                combine(G - 1)
                overflow(l)

            def overflow(l):
                dve.wait_ge(sem("m_ovi"), l + 1)
                over = dve.value_load(OVI[0:1, l, 0:1], min_val=0, max_val=1)
                with dve.If(over > 0):
                    olink = linker(dve, f"ov{l}_step")
                    mine = MIN_.rearrange("p (i g) -> p i g", i=2)
                    olink(tt(mine, MOH.rearrange("p (i g) -> p i g", i=2), bc(MOV, 1, [P, 2, G]), MUL))
                    olink(tt(MPO, MPO, MIN_, MUL))
                    olink(total(MKO, MPO.rearrange("p (i g) -> p i g", i=2)))
                    olink(total(MOF, mine))
                    olink(ts(MOF, MOF, 1e6, MUL, -1e6 - P, ADD))
                    olink(tt(MKO, MKO, MOF, ADD))
                    for i in range(NT):
                        src = MGT[:, 32 * i:32 * i + 32].rearrange("p (g e) -> p e g", g=G)
                        dst = MR1[:, 32 * i:32 * i + 32].rearrange("p (e g) -> p e g", g=G)
                        olink(tt(dst, src, bc(MIN_[:, 4 * i:4 * i + 4], 1, [P, E, G]), MUL))
                        olink(total(MGO[:, 8 * i:8 * i + 8], dst))
                    dve.wait_ge(sem("comb_x"), 16 * (l + 1))
                    for i in range(NT):
                        done(tt(PF[:, i, 0, :], CT[:, C_IOTA:C_IOTA + P], MKO[:, i:i + 1].to_broadcast([P, P]),
                                ALU.is_equal), f"ov{l}_dve")
                    done(nc.vector.memset(YS[:, :], 0.0), f"ov{l}_dve")
                    dve.wait_ge(sem(f"ov{l}_pe"), 2)
                    olink(nc.vector.tensor_copy(GG[:, 0:E], PS[:, 4, 0:E]))
                    for b in range(2):
                        dve.wait_ge(sem(f"ov{l}_act"), 3 + b)
                        done(tt(GTL[:, 0, 4 * b:4 * b + 4, :], PS[:, 5 + b, :].rearrange("p (k j) -> p k j", k=4),
                                GTH[:, 0, 4 * b:4 * b + 4, :].bitcast(F32), SUB), f"ov{l}_dve")
                    dve.wait_ge(sem(f"ov{l}_dve"), 5)
                    done(nc.vector.memset(MR1[:, 0:1], 0.0), f"ov{l}_dve")
                    with dve.Fori(0, E) as e:
                        for j in range(3):
                            dve.wait_ge(sem(f"ov{l}_act"), 5 * e + 5 + j)
                            raw, hi, lo = overflow_views(j)
                            done(tt(lo, raw, hi.bitcast(F32), SUB), f"ov{l}_dve")
                        dve.wait_ge(sem(f"ov{l}_act"), 5 * e + 8)
                        done(stt(HID[:, 0, :], SIL[:, 0, :], GG[:, bass.ds(e, 1)], PS[:, 0, P:2 * P], MUL, MUL), f"ov{l}_dve")
                        dve.wait_ge(sem(f"ov{l}_act"), 5 * e + 9)
                        done(tt(HIL[:, 0, :], PS[:, 2, 0:P], HIH[:, 0, :].bitcast(F32), SUB), f"ov{l}_dve")
                        dve.wait_ge(sem(f"ov{l}_pe"), 3 * e + 7)
                        done(tt(YS[:, :], PS[:, 3:5, :].rearrange("p a n -> p (a n)"), YS[:, :], ADD), f"ov{l}_dve")
                    for i in range(NT):
                        for b in range(2):
                            dve.wait_ge(sem(f"ov{l}_pe"), 3 * E + 5 + 2 * i + b)
                            xs = X[:, i, 512 * b:512 * b + 512]
                            ins = tt(xs, PS[:, 3 + 2 * i + b, :], xs, ADD)
                    done(ins, f"ov{l}_dve")
                    dve.wait_ge(sem(f"ov{l}_dve"), OV_DVE)
                dve.end_ifs()

            norm(0)
            dve.wait_ge(sem("pt"), 1)
            lv = PT[:, 48:60].rearrange("p (l h) -> p l h", l=3)
            le = LBE.rearrange("p (l h) -> p l h", l=3)
            link(tt(LBM, lv[:, 0, :], lv[:, 1, :], ALU.max))
            link(tt(LBM, LBM, lv[:, 2, :], ALU.max))
            done(tt(le, lv, bc(LBM, 1, [P, 3, 4]), SUB), "lb_d")

            def layer0_early(c):
                if c == 0:
                    dve.wait_ge(sem("lb_e"), 1)
                    link(tt(LBS, le[:, 0, :], le[:, 1, :], ADD))
                    link(tt(LBS, LBS, le[:, 2, :], ADD))
                    link(nc.vector.reciprocal(LBS, LBS))
                    link(tt(LBM, le[:, 0, :], LBS, MUL))
                    link(ts(LBC, LBM, -0.5, MUL, 0.5, ADD))
                    link(ts(LBO, LBM, 0.5, MUL, 0.5, ADD), also="lb")
                    link(ts(LBH, LBC, 0.5, MUL))
                    link(ts(LBN, LBC, -0.5, MUL))
                if c == 4:
                    dve.wait_ge(sem("proj_ev"), outs_before[0, "in", 3])
                    link(stt(TQ[:, :, :], TQ[:, :, :], 1.0, QR[:, :, :], ADD, MUL))
                    for h in range(4):
                        link(ts(KH[:, h, :], TF[:, h, :], LBN[:, h:h + 1], MUL, LBH[:, h:h + 1], ADD), also="b_kh")

            in_projection(0, layer0_early)
            chunk_done(dve, 0, "in", len(CHUNKS[0]) - 1)
            dve.wait_ge(sem("proj_ev"), proj_total[0])
            sqa = H[:, :, 0:640]
            link(tt(sqa, TA[:, :, 0:640], TA[:, :, 0:640], MUL))
            for i in range(NT):
                ins = total(ASS[:, 10 * i:10 * i + 10], H[:, i, 0:640].rearrange("p (h n) -> p h n", n=64))
                if i:
                    done(ins, "sumsq")
            dve.wait_ge(sem("root"), 1)
            for i in range(NT):
                q = TA[:, i, 0:512].rearrange("p (h n) -> p h n", n=64)
                done(tt(q, q, bc(ARS[:, 10 * i:10 * i + 8], 2, [P, 8, 64]), MUL), "a_qk")
                k = TA[:, i, 512:640].rearrange("p (g n) -> p g n", n=64)
                rs = bc(ARS[:, 10 * i + 8:10 * i + 10], 2, [P, 2, 64])
                for d in range(2):
                    done(tt(KD[:, i, :, d, :], k, rs, MUL), "a_qk")
            nc.vector.tensor_copy(VS[0:64, :], TA[0:64, 1, 640:768])
            done(nc.vector.tensor_copy(VS[64:128, :], TA[64:128, 0, 640:768]), "a_vs")
            dve.wait_ge(sem("b_ln"), 4)
            dve.wait_ge(sem("b_rst"), 1)
            bf = LB[:, :, :].rearrange("p h t -> p (h t)")
            done(nc.vector.tensor_tensor_scan(out=bf, data0=RST[:, :], data1=bf, initial=0.0, op0=MUL, op1=ADD), "b_scan")
            dve.wait_ge(sem("b_mm"), 1)
            at8 = AT[:, :, :, :].rearrange("p i h t -> p (i h) t")
            done(tt(at8, PS[:, 4:6, :].rearrange("p i (h t) -> p (i h) t", h=4), bc(ident, 1, [P, 8, P]), MUL), "b_cp")

            def b_factors(L):
                dve.wait_ge(sem("b_e"), L)
                if L >= 3:
                    dve.wait_ge(sem("b_mm"), L - 1)
                c = 2 ** L
                ev, mv, qv, kv = (a.rearrange("p (n c) -> p n c", c=c) for a in (
                    DL[:, L % 2, :], ML[:, L % 2, :], TQ[:, :, :].rearrange("p h t -> p (h t)"),
                    KH[:, :, :].rearrange("p h t -> p (h t)")))
                tt(mv[:, :, c // 2:], ev[:, :, c // 2:], qv[:, :, c // 2:], MUL)
                done(tt(mv[:, :, 0:c // 2], ev[:, :, 0:c // 2], kv[:, :, 0:c // 2], MUL), "b_ml")

            def b_place(L):
                dve.wait_ge(sem("b_mm"), L + 1)
                dve.wait_ge(sem("b_cp"), L)
                b = 4 + 2 * (L % 2)
                done(nc.vector.copy_predicated(at8, bc(mask(L - 1), 1, [P, 8, P]),
                                               PS[:, b:b + 2, :].rearrange("p i (h t) -> p (i h) t", h=4)), "b_cp")

            b_factors(1)
            b_factors(2)
            sk = SINK.rearrange("p (a b) -> p b a", b=2)
            for i in range(NT):
                dve.wait_ge(sem("a_SB"), i + 1)
                mx = AMX[:, 8 * i:8 * i + 8]
                link(total(mx, SB[:, i, :, :], ALU.max))
                mx4 = mx.rearrange("p (b a) -> p b a", b=2)
                link(tt(mx4, mx4, sk, ALU.max))
                done(tt(ASM[:, 8 * i:8 * i + 8].rearrange("p (b a) -> p b a", b=2), sk, mx4, SUB), "a_sm")
                done(tt(SB[:, i, :, :], SB[:, i, :, :], bc(mx, 2, [P, 8, P]), SUB), "a_D")
            b_place(1)
            b_factors(3)
            b_place(2)
            for i in range(NT):
                dve.wait_ge(sem("a_P"), i + 1)
                link(total(ADEN[:, 8 * i:8 * i + 8], SB[:, i, :, :]))
            dve.wait_ge(sem("a_es"), 1)
            link(tt(ADEN, ADEN, ASM, ADD))
            link(nc.vector.reciprocal(ADEN, ADEN))
            b_factors(4)
            b_place(3)
            for i in range(NT):
                dve.wait_ge(sem("a_O"), i + 1)
                den = ADEN[:, 8 * i:8 * i + 8].rearrange("p (b a) -> p a b", b=2)
                done(tt(TA[:, i, 0:512].rearrange("p (a b n) -> p a b n", b=2, n=64),
                        PS[:, i, :].rearrange("p (a b n) -> p a b n", b=2, n=64), bc(den, 3, [P, 4, 2, 64]), MUL), "a_mix")
            for L in (5, 6):
                b_factors(L)
                b_place(L - 1)
            b_factors(7)
            b_place(6)
            b_factors(8)
            dve.wait_ge(sem("b_tg"), 1)
            link(stt(TG[:, :, :], TG[:, :, :], 1.0, TB[:, :, 512:], ADD, MUL))
            g8 = TG[:, :, :].rearrange("p i (h n) -> p (i h) n", n=P)
            link(stt(g8, g8, 0.5, bc(BGAIN, 1, [P, 8, P]), MUL, MUL))
            dve.wait_ge(sem("b_sq"), 1)
            done(total(BSS, SQB[:, :, :, :].rearrange("p i h n -> p (i h) n")), "sumsq")
            dve.wait_ge(sem("root"), 2)
            o8 = PS[:, 6:8, :].rearrange("p i (h n) -> p (i h) n", n=P)
            sq8 = SQB[:, :, :, :].rearrange("p i h n -> p (i h) n")
            link(tt(sq8, o8, bc(BRS, 2, [P, 8, P]), MUL))
            done(tt(TB[:, :, 512:], SQB[:, :, :, :].rearrange("p i h n -> p i (h n)"), TG[:, :, :], MUL), "mix")
            out_projection(0)
            if stop == 1:
                return
            norm(1)
            moe(0)
            if stop == 2:
                return
            norm(2)

            def conv(c):
                dve.wait_ge(sem("proj_ev"), outs_before[1, "in", c] + 3)
                for tap in range(4):
                    for b in range(3 * c, 3 * c + 3):
                        w = PT[:, tap * 12 + b:tap * 12 + b + 1]
                        src = CB[:, b, tap:tap + T]
                        if tap == 0:
                            ins = ts(SL[:, b, :], src, w, MUL)
                        else:
                            ins = stt(SL[:, b, :], src, w, SL[:, b, :], MUL, ADD)
                        if tap == 3:
                            done(ins, "c_conv")
                        elif b == 3 * c + 2:
                            link(ins)

            def conv_silu(c):
                dve.wait_ge(sem("c_tanh"), c + 1)
                s3 = SL[:, 3 * c:3 * c + 3, :]
                done(stt(s3, CB[:, 3 * c:3 * c + 3, 0:T], 1.0, s3, ADD, MUL), "c_silu")

            def layer1_early(c):
                if 1 <= c <= 4:
                    conv(c - 1)
                if 3 <= c <= 6:
                    conv_silu(c - 3)

            in_projection(1, layer1_early)
            dve.wait_ge(sem("proj_ev"), proj_total[1])
            dve.wait_ge(sem("c_bt"), 1)
            link(ts(BH, BT2, 0.25, MUL, 0.25, ADD))
            a3 = XA.rearrange("p (i h) -> p i h", i=2)
            link(tt(a3, TM[:, :, 520:528], bc(DTB, 1, [P, 2, 8]), ADD), also="c_xa")
            link(stt(XB_, XA, -1.0, XA, MUL, ALU.max), also="c_xa")
            dve.wait_ge(sem("c_sp"), 1)
            link(stt(XE, XA, 0.0, XE, ALU.max, ADD))
            dve.wait_ge(sem("c_ea"), 1)
            done(stt(GL.rearrange("p (i h) -> p i h", i=2), XE.rearrange("p (i h) -> p i h", i=2), -1.0,
                     bc(EA, 1, [P, 2, 8]), MUL, MUL), "c_gl")
            dve.wait_ge(sem("c_st"), 1)
            done(ts(CSS, PS[:, 2, 0:32], 0.25, MUL, EPS, ADD), "sumsq")
            dve.wait_ge(sem("root"), 3)
            rk = CRK.rearrange("p (i n) -> p i n", i=2)
            bh = BH.rearrange("p (i h) -> p i h", i=2)
            dve.wait_ge(sem("h"), 3)
            link(ts(RBV[:, :, 0:8], rk[:, :, 0:8], 0.5 * 0.125, MUL), also="c_rb")
            link(ts(RBV[:, :, 8:16], rk[:, :, 8:16], 0.5, MUL), also="c_rb")
            link(tt(RBV[:, :, 16:24], rk[:, :, 8:16], bh, MUL), also="c_rb")
            dve.wait_ge(sem("c_b"), 1)
            link(nc.vector.tensor_copy(BCOL, PS[:, 3, 0:24]))
            dve.wait_ge(sem("c_row"), 1)
            rows = [PS[:, 4 + 2 * i:6 + 2 * i, :].rearrange("p a (h t) -> p (a h) t", t=P) for i in range(2)]
            tri = [GA[:, :, 0:P], GA[:, :, 2 * P:3 * P]]
            for i in range(NT):
                link(tt(tri[i], rows[i], bc(BCOL[:, 8 * i:8 * i + 8], 2, [P, 8, P]), SUB))
            done(tt(GA[:, :, P:2 * P], rows[1], bc(BCOL[:, 16:24], 2, [P, 8, P]), ADD), "c_ga")
            for i in range(NT):
                done(tt(tri[i], tri[i], bc(CT[:, C_NEG:C_NEG + P], 1, [P, 8, P]), ALU.min), "c_ga")
            dve.wait_ge(sem("d_S"), 1)
            dec = CT[:, C_DEC:C_DEC + 4 * T].rearrange("p (h t) -> p h t", h=4)
            done(tt(ATD[:, :, 0:T], PS[:, 2:6, 0:T], dec, MUL), "d_at")
            done(tt(ATD[:, :, T:384], PS[:, 2:6, T:384], dec[:, :, 0:P], MUL), "d_at")
            dve.wait_ge(sem("c_kb"), 1)
            for n, (dst, src) in enumerate(((QH, SL[:, 0:4, :]), (KHC, SL[:, 4:8, :]), (KB, SL[:, 4:8, :]))):
                done(tt(dst[:, :, :], src, PS[:, 2 * n:2 * n + 2, :].rearrange("p a (b t) -> p (a b) t", t=T), MUL), "c_qk")
            dve.wait_ge(sem("d_O"), 2)
            o8 = PS[:, 6:8, :].rearrange("p i (h n) -> p (i h) n", n=P)
            xc8 = QRD[:, :, :, :].rearrange("p i h n -> p (i h n)").rearrange("p (a n) -> p a n", n=P)
            link(total(DMU, o8))
            link(ts(DMU, DMU, 1.0 / P, MUL))
            done(tt(xc8, o8, bc(DMU, 2, [P, 8, P]), SUB), "d_xc")
            dve.wait_ge(sem("c_vt"), 1)
            for i in range(NT):
                done(tt(VB[:, i, :, :], PS[:, 6 + i, :].rearrange("p (h n) -> p h n", h=8),
                        bc(bh[:, i, :], 2, [P, 8, 64]), MUL), "c_vb")
            dve.wait_ge(sem("c_gexp"), 1)
            for half in range(2):
                dve.wait_ge(sem("c_kk"), half + 1)
                b = 4 * half
                hs = slice(4 * half, 4 * half + 4)
                done(stt(NTD[:, hs, :], PS[:, b:b + 4, 0:384], -1.0, GA[:, hs, :], MUL, MUL), "c_nt")
            done(nc.vector.tensor_copy(YI[:, :, :, :].rearrange("p i h t -> p (i h) t"), bc(ident, 1, [P, 16, P])), "c_yi")
            dve.wait_ge(sem("c_yi"), 1)

            def y_group(gr):
                return YI[:, gr // 2, 4 * (gr % 2):4 * (gr % 2) + 4, :]

            for gr in range(4):
                i, h0 = gr // 2, 4 * (gr % 2)
                done(nc.vector.copy_predicated(y_group(gr), bc(mask(0), 1, [P, 4, P]),
                                               NTD[:, h0:h0 + 4, 2 * P * i:2 * P * i + P]), "c_Y")
            for half in range(2):
                dve.wait_ge(sem("c_qkp"), half + 1)
                hs = slice(4 * half, 4 * half + 4)
                done(tt(ATC[:, hs, :], PS[:, 4 * half:4 * half + 4, 0:384], GA[:, hs, :], MUL), "c_at")

            def inverse_level(L):
                for gr in range(4):
                    dve.wait_ge(sem("c_Z"), 4 * (L - 1) + gr + 1)
                    done(nc.vector.copy_predicated(y_group(gr), bc(mask(L), 1, [P, 4, P]),
                                                   PS[:, 2 * gr + 1, :].rearrange("p (h t) -> p h t", h=4)), "c_Y")

            inverse_level(1)
            dve.wait_ge(sem("d_sq"), 1)
            done(total(DSS, SQD[:, :, :].rearrange("p i (h n) -> p (i h) n", n=P)), "sumsq")
            dve.wait_ge(sem("root"), 4)
            link(tt(xc8, xc8, bc(DRS, 2, [P, 8, P]), MUL))
            inverse_level(2)
            dve.wait_ge(sem("dg_in"), 32)
            xc2 = QRD[:, :, :, :].rearrange("p i h n -> p i (h n)")
            link(tt(xc2, xc2, bc(DG[:, :], 1, [P, 2, 512]), MUL))
            link(tt(xc2, xc2, bc(DB[:, :], 1, [P, 2, 512]), ADD))
            inverse_level(3)
            dve.wait_ge(sem("d_tg"), 1)
            tg = TMP[:, :, :, :].rearrange("p i h n -> p i (h n)")
            link(stt(tg, tg, 1.0, TM[:, :, 1552:2064], ADD, MUL))
            done(stt(TM[:, :, 1552:2064], xc2, 0.5, tg, MUL, MUL), "d_mix")
            inverse_level(4)
            dve.wait_ge(sem("c_tz"), 1)
            link(stt(SG[:, :, :], SG[:, :, :], 1.0, TM[:, :, 0:512], ADD, MUL))
            g16 = SG[:, :, :].rearrange("p i (h n) -> p (i h) n", n=64)
            link(stt(g16, g16, 0.5, bc(CGAIN, 1, [P, 16, 64]), MUL, MUL))
            inverse_level(5)
            inverse_level(6)
            dve.wait_ge(sem("c_R"), 1)
            done(tt(R1[:, :, :], PS[:, 1, :].rearrange("p (h n) -> p h n", h=8), VB[:, 1, :, :], ADD), "c_R1")
            dve.wait_ge(sem("c_osq"), 1)
            sc = SQC[:, 0:4, :].rearrange("p a n -> p (a n)")
            sc16 = sc.rearrange("p (a n) -> p a n", n=64)
            done(total(COS_, sc16), "sumsq")
            dve.wait_ge(sem("root"), 5)
            link(tt(sc16, PS[:, 3:5, :].rearrange("p i (h n) -> p (i h) n", n=64), bc(COS_, 2, [P, 16, 64]), MUL))
            done(tt(TM[:, :, 0:512], sc.rearrange("p (i n) -> p i n", i=2), SG[:, :, :], MUL), "mix")
            out_projection(1)
            if stop == 3:
                return
            norm(3)
            moe(1)

        @block.tensor
        def _(pe):
            mm = nc.tensor.matmul

            def transposes(b, dst_src, name):
                for dst, src in dst_src:
                    last = nc.tensor.transpose(dst, src, ident)
                done(last, name)

            def lhs(n, src):
                for b in range(4):
                    transposes(b, [(PS[:, b, kk * T + i * P:kk * T + i * P + P], src(i, 2 * b + kk))
                                   for kk in range(2) for i in range(NT)], "hT_ps")

            def in_projection(layer):
                pe.wait_ge(sem("h"), 2 * layer + 1)
                lhs(2 * layer, lambda i, k: H[:, i, k * P:(k + 1) * P])
                pe.wait_ge(sem("hT_lo"), 8 * layer + 4)
                for c in range(len(CHUNKS[layer])):
                    project(pe, layer, "in", c, None)

            def out_projection(layer, src):
                lhs(2 * layer + 1, src)
                pe.wait_ge(sem("hT_lo"), 8 * layer + 8)
                for c in range(3):
                    project(pe, layer, "out", c, None)

            def moe(l):
                pe.wait_ge(sem("h"), 2 * l + 2)
                hk = H[:, :, :].rearrange("p i (q k) -> p i k q", k=KT)
                for b in range(4):
                    transposes(b, [(PS[:, b, kk * T + i * P:kk * T + i * P + P], hk[:, i, 2 * b + kk, :])
                                   for kk in range(2) for i in range(NT)], "m_T")
                pe.wait_ge(sem("m_ht"), 4 * l + 4)
                pe.wait_ge(sem("rw_in"), 64)
                for i in range(NT):
                    for k in range(KT):
                        last = mm(PS[:, 4, 36 * i:36 * i + 36], HTF[:, k, i * P:(i + 1) * P], RW[:, l, k, :],
                                  start=k == 0, stop=k == KT - 1)
                done(last, "m_lg")
                pe.wait_ge(sem("m_rank"), 2 * l + 1)
                oh = MOH.rearrange("p (i g) -> p i g", i=2)
                mm(PS[:, 5, 0:4], CT[:, C_STRIU:C_STRIU + P], oh[:, 0], start=True, stop=True)
                mm(PS[:, 5, 4:8], CT[:, C_ONES:C_ONES + P], oh[:, 0], start=True, stop=False)
                mm(PS[:, 5, 4:8], CT[:, C_STRIU:C_STRIU + P], oh[:, 1], start=False, stop=True)
                mm(PS[:, 5, 8:12], CT[:, C_ONES:C_ONES + P], oh[:, 0], start=True, stop=False)
                done(mm(PS[:, 5, 8:12], CT[:, C_ONES:C_ONES + P], oh[:, 1], start=False, stop=True), "m_pos")
                pe.wait_ge(sem("m_pf"), 2 * l + 2)
                for g in range(G):
                    for i in range(NT):
                        last = nc.tensor.transpose(PS[:, 1 + g // 2, (g % 2) * T + i * P:(g % 2) * T + i * P + P],
                                                   PF[:, i, g, :], ident)
                done(last, "m_pt")
                pe.wait_ge(sem("m_gate"), l + 1)
                gt = MGT.rearrange("p (i n) -> p i n", i=2)
                for g in range(G):
                    for i in range(NT):
                        last = mm(PS[:, 4, 8 * g:8 * g + 8], PF[:, i, g, :], gt[:, i, 8 * g:8 * g + 8],
                                  start=i == 0, stop=i == NT - 1)
                done(last, "m_gg")

                def gather(g):
                    for b in range(2):
                        if g:
                            pe.wait_ge(sem("g_lo"), 8 * l + 2 * g - 1 + b)
                        for kk in range(4):
                            k = 4 * b + kk
                            ps = PS[:, 5 + b, kk * P:(kk + 1) * P]
                            for n, (part, i) in enumerate((a, i) for a in (HH, HL) for i in range(NT)):
                                rows = part[:, i, :].rearrange("p (q k) -> p k q", k=KT)[:, k, :]
                                last = mm(ps, rows, PR[:, i, g, :], start=n == 0, stop=n == 3)
                        done(last, "g_ps")

                def gate_up(n):
                    if n >= 2:
                        pe.wait_ge(sem("hid"), 32 * l + n - 1)
                    for j in range(2):
                        u = unit_of[l, "moe", n] + j
                        pe.wait_ge(sem("unit_lo"), u + 1)
                        wh, wl = (w[:, u % UNITS, :].rearrange("p (m k n) -> p k m n", m=2, k=4) for w in (WH, WL))
                        for kk in range(4):
                            k = 4 * j + kk
                            last = product(PS[:, n % 2, 0:2 * P], GTH[:, (n // E) % 2, k, :], GTL[:, (n // E) % 2, k, :],
                                           wh[:, kk], wl[:, kk], k == 0, k == KT - 1)
                        done(last, "unit_used")

                def hid_T(n):
                    pe.wait_ge(sem("hid"), 32 * l + n + 1)
                    if n >= 2:
                        pe.wait_ge(sem("hid_lo"), 32 * l + n - 1)
                    done(nc.tensor.transpose(PS[:, 2, (n % 2) * P:(n % 2) * P + P], HID[:, n % 2, :], ident), "hid_T")

                def down(n):
                    u = unit_of[l, "moe", n] + 2
                    pe.wait_ge(sem("hid_lo"), 32 * l + n + 1)
                    if n % E == 0 and n:
                        pe.wait_ge(sem("y_sb"), 4 * l + n // E)
                    for b in range(2):
                        cs = slice(512 * b, 512 * b + 512)
                        last = product(PS[:, 3 + b, :], HIH[:, n % 2, :], HIL[:, n % 2, :],
                                       WH[:, u % UNITS, cs], WL[:, u % UNITS, cs], n % E == 0, n % E == E - 1)
                    done(last, "unit_used")

                def combine(g):
                    pe.wait_ge(sem("y_sb"), 4 * l + g + 1)
                    for i in range(NT):
                        for b in range(2):
                            c = 4 * (4 * l + g) + 2 * i + b
                            if c:
                                pe.wait_ge(sem("comb_x"), c)
                            done(mm(PS[:, 7, :], PTR[:, g, i * P:(i + 1) * P], YS[:, 512 * b:512 * b + 512],
                                    start=True, stop=True), "comb")

                pe.wait_ge(sem("m_pr"), l + 1)
                pe.wait_ge(sem("m_hl"), l + 1)
                gather(0)
                pe.wait_ge(sem("m_ptr"), l + 1)
                pe.wait_ge(sem("m_ggs"), l + 1)
                for n in range(G * E + 1):
                    if n < G * E:
                        if n % E == 0:
                            pe.wait_ge(sem("g_lo"), 8 * l + 2 * (n // E) + 2)
                        gate_up(n)
                    if n:
                        if n % E == 6 and n // E < G - 1:
                            gather(n // E + 1)
                        hid_T(n - 1)
                        down(n - 1)
                        if n > E and n % E == 1:
                            pass
                    if n > 1 and n % E == 1:
                        combine(n // E - 1)
                combine(G - 1)
                overflow(l)

            def overflow(l):
                pe.wait_ge(sem("m_ovi"), l + 1)
                over = pe.value_load(OVI[0:1, l, 0:1], min_val=0, max_val=1)
                with pe.If(over > 0):
                    pe.wait_ge(sem("comb_x"), 16 * (l + 1))
                    pe.wait_ge(sem(f"ov{l}_dve"), 2)
                    transposes(1, [(PS[:, 1, i * P:(i + 1) * P], PF[:, i, 0, :]) for i in range(NT)], f"ov{l}_pe")
                    for i in range(NT):
                        last = mm(PS[:, 4, 0:E], PF[:, i, 0, :], MGO[:, E * i:E * i + E], start=i == 0, stop=i == NT - 1)
                    done(last, f"ov{l}_pe")
                    pe.wait_ge(sem(f"ov{l}_act"), 1)
                    for b in range(2):
                        for kk in range(4):
                            for n, (part, i) in enumerate((a, i) for a in (HH, HL) for i in range(NT)):
                                rows = part[:, i, :].rearrange("p (q k) -> p k q", k=KT)[:, 4 * b + kk, :]
                                last = mm(PS[:, 5 + b, kk * P:(kk + 1) * P], rows, PR[:, i, 0, :], start=n == 0, stop=n == 3)
                        done(last, f"ov{l}_pe")
                    pe.wait_ge(sem(f"ov{l}_dve"), 5)
                    with pe.Fori(0, E) as e:
                        pe.wait_ge(sem(f"ov{l}_dve"), 6 * e + 9)
                        for k in range(KT):
                            wh, wl = (w[:, k // 4, :].rearrange("p (m k n) -> p k m n", m=2, k=4)[:, k % 4] for w in (WH, WL))
                            last = product(PS[:, 0, 0:2 * P], GTH[:, 0, k, :], GTL[:, 0, k, :], wh, wl, k == 0, k == KT - 1)
                        done(last, f"ov{l}_pe")
                        pe.wait_ge(sem(f"ov{l}_dve"), 6 * e + 10)
                        done(nc.tensor.transpose(PS[:, 2, 0:P], HID[:, 0, :], ident), f"ov{l}_pe")
                        pe.wait_ge(sem(f"ov{l}_dve"), 6 * e + 11)
                        for b in range(2):
                            cs = slice(512 * b, 512 * b + 512)
                            last = product(PS[:, 3 + b, :], HIH[:, 0, :], HIL[:, 0, :], WH[:, 2, cs], WL[:, 2, cs], True, True)
                        done(last, f"ov{l}_pe")
                    pe.wait_ge(sem(f"ov{l}_dve"), 6 * E + 6)
                    pe.wait_ge(sem(f"ov{l}_act"), 2)
                    for i in range(NT):
                        for b in range(2):
                            done(mm(PS[:, 3 + 2 * i + b, :], PTR[:, 0, i * P:(i + 1) * P], YS[:, 512 * b:512 * b + 512],
                                    start=True, stop=True), f"ov{l}_pe")
                    pe.wait_ge(sem(f"ov{l}_dve"), OV_DVE)
                pe.end_ifs()

            pe.wait_ge(sem("ct_in"), 16)
            pe.wait_ge(sem("par_in"), 16 * N_PAR)
            done(nc.tensor.transpose(PS[:, 7, 0:62], ROWS[0:62, :], ident[0:62, 0:62]), "pt_ps")
            in_projection(0)
            pe.wait_ge(sem("proj_ev"), proj_total[0])
            pe.wait_ge(sem("a_qk"), 6)
            for n in range(2):
                transposes(n, [(PS[:, n, a * T + i * P:a * T + i * P + P], TA[:, i, (2 * n + a) * P:(2 * n + a + 1) * P])
                               for a in range(2) for i in range(NT)], "a_T")
            transposes(2, [(PS[:, 2, g * T + i * P:g * T + i * P + P], KD[:, i, g, :, :].rearrange("p d n -> p (d n)"))
                           for g in range(2) for i in range(NT)], "a_T")
            pe.wait_ge(sem("b_kh"), 4)
            for i in range(NT):
                for h in range(4):
                    last = mm(PS[:, 4 + i, h * P:(h + 1) * P], KH[:, h, i * P:(i + 1) * P], TQ[:, h, i * P:(i + 1) * P],
                              start=True, stop=True)
            done(last, "b_mm")
            pe.wait_ge(sem("a_QT"), 3)
            for i in range(NT):
                for par in range(2):
                    r = slice(64 * par, 64 * par + 64)
                    for half in range(2):
                        c = 2 * i + half
                        for a in range(4):
                            q = QT[r, a, c * CH:(c + 1) * CH]
                            ps = PS[64 * half:64 * half + 64, 2 * i + par, a * P:(a + 1) * P]
                            g = (2 * a + par) // 4
                            if half:
                                last = mm(ps, q, KTT[r, g, (c - 1) * CH:(c + 1) * CH], start=True, stop=True)
                            else:
                                mm(ps[:, 0:CH], q, KTT[r, g, c * CH:(c + 1) * CH], start=True, stop=True)
                                if c:
                                    mm(ps[:, CH:], q, KTT[r, g, (c - 1) * CH:c * CH], start=True, stop=True)
                done(last, "a_S")

            def b_level(L):
                pe.wait_ge(sem("b_ml"), L)
                if L >= 2:
                    pe.wait_ge(sem("b_cp"), L - 1)
                b = 4 + 2 * (L % 2)
                m = ML[:, L % 2, :]
                for i in range(NT):
                    for h in range(4):
                        fr = m[:, h * T + i * P:h * T + (i + 1) * P]
                        last = mm(PS[:, b + i, h * P:(h + 1) * P], fr, fr, start=True, stop=True)
                done(last, "b_mm")

            b_level(1)
            b_level(2)
            for i in range(NT):
                pe.wait_ge(sem("a_P"), i + 1)
                for b in range(2):
                    transposes(b, [(PS[:, 2 * i + b, h * P:(h + 1) * P], SB[:, i, 4 * b + h, :]) for h in range(4)], "a_PT")
            b_level(3)
            pe.wait_ge(sem("a_PTS"), 4)
            pe.wait_ge(sem("a_vs"), 1)
            for i in range(NT):
                for half in range(2):
                    for h in range(8):
                        g = h // 4
                        v = VS if (i, half) == (1, 0) else TA[:, i, 640:768]
                        last = mm(PS[64 * half:64 * half + 64, i, h * 64:(h + 1) * 64],
                                  PTS[:, i, 4 * (h % 2) + h // 2, half * 64:half * 64 + 64], v[:, g * 64:(g + 1) * 64],
                                  start=True, stop=True)
                done(last, "a_O")
            for L in (4, 5, 6):
                b_level(L)
            pe.wait_ge(sem("b_ml"), 7)
            pe.wait_ge(sem("b_cp"), 6)
            for i in range(NT):
                for h in range(4):
                    o = h * T + i * P
                    last = mm(PS[0:64, 6, (4 * i + h) * CH:(4 * i + h + 1) * CH], ML[:, 1, o:o + CH], ML[:, 1, o + CH:o + P],
                              start=True, stop=True)
            done(last, "b_mm")
            pe.wait_ge(sem("b_ml"), 8)
            pe.wait_ge(sem("b_cp"), 7)
            for h in range(4):
                last = mm(PS[:, 4, h * P:(h + 1) * P], ML[:, 0, h * T:h * T + P], ML[:, 0, h * T + P:(h + 1) * T],
                          start=True, stop=True)
            done(last, "b_mm")
            pe.wait_ge(sem("b_off"), 2)
            for i in range(NT):
                for h in range(4):
                    hs = slice(h * P, (h + 1) * P)
                    last = mm(PS[:, 6 + i, hs], AT[:, i, h, :], TB[:, i, hs], start=True, stop=i == 0)
                    if i:
                        last = mm(PS[:, 6 + i, hs], AXB[:, h, :], TB[:, 0, hs], start=False, stop=True)
                done(last, "b_O")
            pe.wait_ge(sem("a_mix"), 2)
            pe.wait_ge(sem("mix"), 1)
            out_projection(0, lambda i, k: (TA[:, i, k * P:(k + 1) * P] if k < 4 else TB[:, i, k * P:(k + 1) * P]))
            if stop == 1:
                return
            moe(0)
            if stop == 2:
                return
            in_projection(1)
            pe.wait_ge(sem("proj_ev"), proj_total[1])
            pe.wait_ge(sem("c_sqc"), 1)
            for i in range(NT):
                for b in range(8):
                    last = mm(PS[:, 2, 16 * i + 2 * b:16 * i + 2 * b + 2], SQC[:, b, i * P:(i + 1) * P],
                              CT[:, C_SEL:C_SEL + 2], start=True, stop=True)
            done(last, "c_st")
            pe.wait_ge(sem("c_gl"), 1)
            gl = GL.rearrange("p (i h) -> p i h", i=2)
            for i in range(NT):
                mm(PS[:, 3, 8 * i:8 * i + 8], CT[:, C_TRIU:C_TRIU + P], gl[:, i, :], start=True, stop=True)
            done(mm(PS[:, 3, 16:24], CT[:, C_SLOW:C_SLOW + P], gl[:, 0, :], start=True, stop=True), "c_b")
            for i in range(NT):
                for h in range(8):
                    last = mm(PS[:, 4 + 2 * i + h // 4, (h % 4) * P:(h % 4 + 1) * P],
                              gl[:, i, h:h + 1].to_broadcast([P, P]), CT[:, C_TRIU:C_TRIU + P], start=True, stop=True)
            done(last, "c_row")
            pe.wait_ge(sem("d_rot"), 4)
            for b in range(2):
                transposes(b, [(PS[:, b, a * T + i * P:a * T + i * P + P],
                                QRD[:, i, 4 * b + 2 * a:4 * b + 2 * a + 2, :].rearrange("p h n -> p (h n)"))
                               for a in range(2) for i in range(NT)], "d_T")
            pe.wait_ge(sem("d_QT"), 2)
            pe.wait_ge(sem("c_ga"), 1)
            for h in range(4):
                r = slice(64 * (h % 2), 64 * (h % 2) + 64)
                k, q = QTD[r, 2 + h // 2, :], QTD[r, h // 2, :]
                mm(PS[:, 2 + h, 0:T], k[:, 0:P], q, start=True, stop=True)
                last = mm(PS[:, 2 + h, T:384], k[:, P:T], q[:, P:T], start=True, stop=True)
            done(last, "d_S")
            pe.wait_ge(sem("d_at"), 2)
            for i in range(NT):
                for h in range(4):
                    hs, vs = slice(h * P, (h + 1) * P), slice(1040 + h * P, 1040 + (h + 1) * P)
                    last = mm(PS[:, 6 + i, hs], ATD[:, h, 256 * i:256 * i + P], TM[:, i, vs], start=True, stop=i == 0)
                    if i:
                        last = mm(PS[:, 6 + i, hs], ATD[:, h, P:2 * P], TM[:, 0, vs], start=False, stop=True)
                done(last, "d_O")
            pe.wait_ge(sem("c_rb"), 3)
            for r in range(3):
                for i in range(NT):
                    last = nc.tensor.transpose(PS[0:8, r // 2, (r % 2) * T + i * P:(r % 2) * T + i * P + P],
                                               RBV[:, i, 8 * r:8 * r + 8], ident)
            done(last, "c_rT")
            pe.wait_ge(sem("c_rkt"), 1)
            for r in range(3):
                for j in range(4):
                    last = mm(PS[:, 2 * r + j // 2, (j % 2) * T:(j % 2) * T + T],
                              CT[0:8, C_HEAD + j * P:C_HEAD + (j + 1) * P], RKT[:, r, :], start=True, stop=True)
            done(last, "c_kb")
            pe.wait_ge(sem("d_xc"), 1)
            for i in range(NT):
                for j in range(4):
                    last = nc.tensor.transpose(PS[:, 6 + i, j * P:(j + 1) * P], SL[:, 8 + j, i * P:(i + 1) * P], ident)
            done(last, "c_vt")
            pe.wait_ge(sem("c_qk"), 3)

            def scores(rhs, name, before, read):
                for half in range(2):
                    if read:
                        pe.wait_ge(sem(read), half + 1)
                    elif half:
                        pe.wait_ge(sem("c_vb"), 2)
                    for h in range(4 * half, 4 * half + 4):
                        r = slice(64 * (h % 2), 64 * (h % 2) + 64)
                        k, q = KHC[r, h // 2, :], rhs[r, h // 2, :]
                        mm(PS[:, h, 0:T], k[:, 0:P], q, start=True, stop=True)
                        last = mm(PS[:, h, T:384], k[:, P:T], q[:, P:T], start=True, stop=True)
                    done(last, name)

            scores(KB, "c_kk", None, None)
            scores(QH, "c_qkp", None, "c_nt")
            for L in range(0, 7):
                def group(gr):
                    return gr // 2, 4 * (gr % 2)
                if L:
                    for gr in range(4):
                        i, h0 = group(gr)
                        pe.wait_ge(sem("c_X"), 4 * (L - 1) + gr + 1)
                        for h in range(4):
                            last = mm(PS[:, 2 * gr, h * P:(h + 1) * P], NTD[:, h0 + h, 256 * i:256 * i + P], XI[:, i, h0 + h, :],
                                      start=True, stop=True)
                        done(last, "c_Q")
                    for gr in range(4):
                        i, h0 = group(gr)
                        pe.wait_ge(sem("c_Qs"), 4 * (L - 1) + gr + 1)
                        if L == 1:
                            pe.wait_ge(sem("c_Y"), 4)
                        for h in range(4):
                            last = mm(PS[:, 2 * gr + 1, h * P:(h + 1) * P], QI[:, i, h0 + h, :], YI[:, i, h0 + h, :],
                                      start=True, stop=True)
                        done(last, "c_Z")
                if L < 6:
                    for gr in range(4):
                        i, h0 = group(gr)
                        pe.wait_ge(sem("c_Y"), 4 * L + gr + 1)
                        if L == 0:
                            pe.wait_ge(sem("c_at"), 2)
                        for h in range(4):
                            last = nc.tensor.transpose(PS[:, 2 * gr, h * P:(h + 1) * P], YI[:, i, h0 + h, :], ident)
                        done(last, "c_T")
            pe.wait_ge(sem("c_Y"), 28)
            for h in range(8):
                last = mm(PS[:, 0, h * 64:(h + 1) * 64], YI[:, 0, h, :], VB[:, 0, h, :], start=True, stop=True)
            done(last, "c_U")
            pe.wait_ge(sem("c_Us"), 1)
            for h in range(8):
                last = mm(PS[:, 1, h * 64:(h + 1) * 64], NTD[:, h, P:2 * P], U[:, 0, h, :], start=True, stop=True)
            done(last, "c_R")
            pe.wait_ge(sem("c_R1"), 1)
            for h in range(8):
                last = mm(PS[:, 2, h * 64:(h + 1) * 64], YI[:, 1, h, :], R1[:, h, :], start=True, stop=True)
            done(last, "c_U")
            for i in range(NT):
                pe.wait_ge(sem("c_Us"), i + 1)
                for h in range(8):
                    hs = slice(h * 64, (h + 1) * 64)
                    last = mm(PS[:, 3 + i, hs], ATC[:, h, 256 * i:256 * i + P], U[:, i, h, :], start=True, stop=i == 0)
                    if i:
                        last = mm(PS[:, 3 + i, hs], ATC[:, h, P:2 * P], U[:, 0, h, :], start=False, stop=True)
                done(last, "c_O")
            pe.wait_ge(sem("d_mix"), 1)
            pe.wait_ge(sem("mix"), 2)
            out_projection(1, lambda i, k: (TM[:, i, k * P:(k + 1) * P] if k < 4 else
                                            TM[:, i, 1552 + (k - 4) * P:1552 + (k - 3) * P]))
            if stop == 3:
                return
            moe(1)


INPUTS = ["x", "mix_norm", "moe_norm", "ev_w_in", "ev_w_out", "a_q_gain", "a_k_gain", "a_sinks", "b_lb_logits",
          "b_out_gain", "od_w_in", "od_w_out", "c_conv_w", "c_a_log", "c_dt_bias", "c_out_gain", "d_out_gain",
          "d_out_bias", "moe_w_rg", "moe_b_rg", "moe_w_re", "moe_b_re", "moe_w_gate", "moe_w_up", "moe_w_down"]
STOP = 4


def kernel(**inputs):
    import concourse.bacc as bacc
    from concourse.bass_utils import run_bass_kernel_spmd

    nc = bacc.Bacc("TRN2", target_bir_lowering=False, num_devices=1)
    arrays = {name: np.ascontiguousarray(inputs[name]) for name in INPUTS}
    arrays["consts"] = constant_table()
    arrays["masks"] = level_masks()
    aps = {name: nc.dram_tensor(name, a.shape, mybir.dt.from_np(a.dtype), kind="ExternalInput").ap()
           for name, a in arrays.items()}
    out = nc.dram_tensor("out", arrays["x"].shape, F32, kind="ExternalOutput").ap()
    program(nc, **aps, out=out, stop=STOP)
    return run_bass_kernel_spmd(nc, [arrays], core_ids=[0]).results[0]["out"]
```
